# Optimizing a Trainium2 kernel written in Bass

```python
import math
import jax
import jax.numpy as jnp
from jax import lax
import numpy as np

D_MODEL = 1024
BATCH = 1
SEQ = 1024
DEPTH = 2

CHUNK = 64
N_MIXERS = 2
N_ATT_LAYERS = (DEPTH + 1) // 2
N_RWKV_LAYERS = DEPTH // 2
N_VRES = max(N_RWKV_LAYERS - 1, 0)

ATT_HEAD_DIM = 64
ATT_Q_HEADS = D_MODEL // ATT_HEAD_DIM
ATT_KV_HEADS = 4
ATT_GROUP = ATT_Q_HEADS // ATT_KV_HEADS
ATT_Q_DIM = ATT_Q_HEADS * ATT_HEAD_DIM
ATT_KV_DIM = ATT_KV_HEADS * ATT_HEAD_DIM
ATT_WINDOW = 128
WINDOW_CHUNKS = ATT_WINDOW // CHUNK
ROPE_THETA = 10000.0
MAX_POS_OFFSET = 4096
NEG_INF = -1e30

RWKV_HEAD = 64
RWKV_HEADS = D_MODEL // RWKV_HEAD
DECAY_LORA = 64
AAA_LORA = 64
MV_LORA = 32
GATE_LORA = 128
GN_EPS = 64e-5

FFN_HIDDEN = ((-(-8 * D_MODEL // 3) + 255) // 256) * 256

EPS = 1e-6

kernel_name = 'hybrid_swa_sink_rwkv7_adaln'

def _rms(x, g):
    xf = x.astype(jnp.float32)
    y = xf * lax.rsqrt(jnp.mean(xf * xf, axis=-1, keepdims=True) + EPS) * g.astype(jnp.float32)
    return y.astype(x.dtype)

def _modulate(h, shift, scale):
    return h * (1.0 + scale[:, None, :]) + shift[:, None, :]

def _rope(x, cos, sin):
    half = x.shape[-1] // 2
    x1, x2 = x[..., :half], x[..., half:]
    c = cos[:, :, None, :]
    s = sin[:, :, None, :]
    return jnp.concatenate([x1 * c - x2 * s, x2 * c + x1 * s], axis=-1)

def _band(t, nc):
    parts = [jnp.pad(t, ((0, 0), (j, 0), (0, 0), (0, 0), (0, 0)))[:, :nc]
             for j in range(WINDOW_CHUNKS - 1, -1, -1)]
    return jnp.concatenate(parts, axis=2)

def _attn_mixer(h, cos, sin, w_in, w_out, q_g, k_g, sinks):
    b, s, _ = h.shape
    nc = s // CHUNK
    qkv = h @ w_in
    q, k, v = jnp.split(qkv, [ATT_Q_DIM, ATT_Q_DIM + ATT_KV_DIM], axis=-1)
    q = q.reshape(b, s, ATT_Q_HEADS, ATT_HEAD_DIM)
    k = k.reshape(b, s, ATT_KV_HEADS, ATT_HEAD_DIM)
    v = v.reshape(b, s, ATT_KV_HEADS, ATT_HEAD_DIM)
    q = _rope(_rms(q, q_g).astype(jnp.float32), cos, sin) * (ATT_HEAD_DIM ** -0.5)
    k = _rope(_rms(k, k_g).astype(jnp.float32), cos, sin)
    q = q.astype(h.dtype).reshape(b, nc, CHUNK, ATT_KV_HEADS, ATT_GROUP, ATT_HEAD_DIM)
    kb = _band(k.astype(h.dtype).reshape(b, nc, CHUNK, ATT_KV_HEADS, ATT_HEAD_DIM), nc)
    vb = _band(v.reshape(b, nc, CHUNK, ATT_KV_HEADS, ATT_HEAD_DIM), nc)
    src = jnp.arange(nc)[:, None] - jnp.arange(WINDOW_CHUNKS - 1, -1, -1)[None, :]
    valid = jnp.repeat(src >= 0, CHUNK, axis=1)
    scores = jnp.einsum('bnqhgd,bnkhd->bnhgqk', q, kb).astype(jnp.float32)
    scores = jnp.where(valid[None, :, None, None, None, :], scores, NEG_INF)
    sink = sinks.astype(jnp.float32).reshape(1, 1, ATT_KV_HEADS, ATT_GROUP, 1, 1)
    m = jnp.maximum(scores.max(axis=-1, keepdims=True), sink)
    p = jnp.exp(scores - m)
    p = p / (p.sum(axis=-1, keepdims=True) + jnp.exp(sink - m))
    o = jnp.einsum('bnhgqk,bnkhd->bnqhgd', p.astype(vb.dtype), vb).reshape(b, s, ATT_Q_DIM)
    return o @ w_out

def _wkv7_scan(r, decay, k, v, kk, a):
    b = r.shape[0]

    def step(state, inp):
        r_t, w_t, k_t, v_t, kk_t, a_t = inp
        sk = jnp.einsum('bhij,bhj->bhi', state, kk_t)
        state = (state * w_t[:, :, None, :]
                 - sk[..., None] * (kk_t * a_t)[:, :, None, :]
                 + v_t[..., None] * k_t[:, :, None, :])
        y = jnp.einsum('bhij,bhj->bhi', state, r_t)
        return state, y

    seqs = tuple(jnp.moveaxis(t, 1, 0) for t in (r, decay, k, v, kk, a))
    s0 = jnp.zeros((b, RWKV_HEADS, RWKV_HEAD, RWKV_HEAD), jnp.float32)
    _, y = lax.scan(step, s0, seqs)
    return jnp.moveaxis(y, 0, 1)

def _rwkv_mixer(h, v_first, mu, w_rkv, w0, w1, w2, a0, a1, a2, g1, g2,
                k_k, k_a, r_k, ln_w, ln_b, w_out, v0=None, v1=None, v2=None):
    b, s, d = h.shape
    f32 = jnp.float32
    xx = jnp.pad(h, ((0, 0), (1, 0), (0, 0)))[:, :-1] - h
    mix = lambda idx: h + xx * mu[idx]
    x_rkv = h[None] + xx[None] * mu[:3, None, None, :]
    r, k, v = jnp.einsum('pbsd,pde->pbse', x_rkv, w_rkv).astype(f32)
    w = -jax.nn.softplus(-(w0 + jnp.tanh(mix(3) @ w1) @ w2).astype(f32)) - 0.5
    a = jax.nn.sigmoid((a0 + (mix(4) @ a1) @ a2).astype(f32))
    g = (jax.nn.sigmoid(mix(5) @ g1) @ g2).astype(f32)
    if v0 is None:
        v_first = v
    else:
        v = v + (v_first - v) * jax.nn.sigmoid((v0 + (x_rkv[2] @ v1) @ v2).astype(f32))
    heads = lambda t: t.reshape(b, s, RWKV_HEADS, RWKV_HEAD)
    kk = heads(k * k_k.astype(f32))
    kk = kk * lax.rsqrt(jnp.maximum(jnp.sum(kk * kk, axis=-1, keepdims=True), 1e-24))
    k = k * (1.0 + (a - 1.0) * k_a.astype(f32))
    decay = jnp.exp(-jnp.exp(w))
    y = _wkv7_scan(heads(r), heads(decay), heads(k), heads(v), kk, heads(a))
    mean = jnp.mean(y, axis=-1, keepdims=True)
    var = jnp.mean(jnp.square(y - mean), axis=-1, keepdims=True)
    y = ((y - mean) * lax.rsqrt(var + GN_EPS)).reshape(b, s, d) * ln_w.astype(f32) + ln_b.astype(f32)
    bonus = jnp.sum(heads(r) * heads(k) * r_k.astype(f32), axis=-1, keepdims=True) * heads(v)
    y = (y + bonus.reshape(b, s, d)) * g
    return y.astype(h.dtype) @ w_out, v_first

def _swiglu(h, w_in, w_out):
    gate, up = jnp.split(h @ w_in, 2, axis=-1)
    return (jax.nn.silu(gate) * up) @ w_out

def setup_inputs(seed: int = 0) -> dict:
    key = jax.random.key(seed)
    ks = iter(jax.random.split(key, 48))
    nrm = lambda shape, scale: jax.random.normal(next(ks), shape, jnp.float32) * scale
    D, F = D_MODEL, FFN_HIDDEN
    NA, NB, NV = N_ATT_LAYERS, N_RWKV_LAYERS, N_VRES
    x = nrm((BATCH, SEQ, D), 1.0)
    c = nrm((BATCH, D), 1.0)
    positions = (jnp.arange(SEQ, dtype=jnp.int32)[None, :]
                 + jax.random.randint(next(ks), (BATCH, 1), 0, MAX_POS_OFFSET, dtype=jnp.int32))
    return {
        'x': x,
        'c': c,
        'positions': positions,
        'ada_w': nrm((DEPTH, D, 6 * D), 0.5 * D ** -0.5),
        'ada_b': nrm((DEPTH, 6 * D), 0.1),
        'norm1_g': 1.0 + nrm((DEPTH, D), 0.1),
        'norm2_g': 1.0 + nrm((DEPTH, D), 0.1),
        'attn_w_in': nrm((NA, D, ATT_Q_DIM + 2 * ATT_KV_DIM), D ** -0.5),
        'attn_w_out': nrm((NA, ATT_Q_DIM, D), ATT_Q_DIM ** -0.5),
        'attn_q_norm': 1.0 + nrm((NA, ATT_HEAD_DIM), 0.1),
        'attn_k_norm': 1.0 + nrm((NA, ATT_HEAD_DIM), 0.1),
        'attn_sinks': nrm((NA, ATT_Q_HEADS), 1.0),
        'rk_mu': jax.random.uniform(next(ks), (NB, 6, D), jnp.float32),
        'rk_w_rkv': nrm((NB, 3, D, D), D ** -0.5),
        'rk_w0': jax.random.uniform(next(ks), (NB, D), jnp.float32, minval=-6.0, maxval=-1.0),
        'rk_w1': nrm((NB, D, DECAY_LORA), D ** -0.5),
        'rk_w2': nrm((NB, DECAY_LORA, D), 0.5 * DECAY_LORA ** -0.5),
        'rk_a0': nrm((NB, D), 0.1),
        'rk_a1': nrm((NB, D, AAA_LORA), D ** -0.5),
        'rk_a2': nrm((NB, AAA_LORA, D), 0.5 * AAA_LORA ** -0.5),
        'rk_v0': nrm((NV, D), 0.1),
        'rk_v1': nrm((NV, D, MV_LORA), D ** -0.5),
        'rk_v2': nrm((NV, MV_LORA, D), 0.5 * MV_LORA ** -0.5),
        'rk_g1': nrm((NB, D, GATE_LORA), D ** -0.5),
        'rk_g2': nrm((NB, GATE_LORA, D), GATE_LORA ** -0.5),
        'rk_k_k': 1.0 + nrm((NB, D), 0.1),
        'rk_k_a': 1.0 + nrm((NB, D), 0.1),
        'rk_r_k': nrm((NB, RWKV_HEADS, RWKV_HEAD), 0.1),
        'rk_ln_w': 1.0 + nrm((NB, D), 0.1),
        'rk_ln_b': nrm((NB, D), 0.01),
        'rk_w_out': nrm((NB, D, D), D ** -0.5),
        'ffn_w_in': nrm((DEPTH, D, 2 * F), D ** -0.5),
        'ffn_w_out': nrm((DEPTH, F, D), F ** -0.5),
    }

def reference(x, c, positions, ada_w, ada_b, norm1_g, norm2_g,
              attn_w_in, attn_w_out, attn_q_norm, attn_k_norm, attn_sinks,
              rk_mu, rk_w_rkv, rk_w0, rk_w1, rk_w2, rk_a0, rk_a1, rk_a2,
              rk_v0, rk_v1, rk_v2, rk_g1, rk_g2, rk_k_k, rk_k_a, rk_r_k,
              rk_ln_w, rk_ln_b, rk_w_out, ffn_w_in, ffn_w_out):
    inv_freq = ROPE_THETA ** (-jnp.arange(0, ATT_HEAD_DIM, 2, dtype=jnp.float32) / ATT_HEAD_DIM)
    ang = positions.astype(jnp.float32)[..., None] * inv_freq
    cos, sin = jnp.cos(ang), jnp.sin(ang)
    c_act = jax.nn.silu(c)
    v_first = None
    for i in range(DEPTH):
        mod = c_act @ ada_w[i] + ada_b[i]
        sh1, sc1, gt1, sh2, sc2, gt2 = jnp.split(mod, 6, axis=-1)
        h = _modulate(_rms(x, norm1_g[i]), sh1, sc1)
        j = i // N_MIXERS
        if i % N_MIXERS == 0:
            y = _attn_mixer(h, cos, sin, attn_w_in[j], attn_w_out[j],
                            attn_q_norm[j], attn_k_norm[j], attn_sinks[j])
        elif j == 0:
            y, v_first = _rwkv_mixer(h, v_first, rk_mu[j], rk_w_rkv[j], rk_w0[j], rk_w1[j], rk_w2[j],
                                     rk_a0[j], rk_a1[j], rk_a2[j], rk_g1[j], rk_g2[j],
                                     rk_k_k[j], rk_k_a[j], rk_r_k[j], rk_ln_w[j], rk_ln_b[j], rk_w_out[j])
        else:
            y, v_first = _rwkv_mixer(h, v_first, rk_mu[j], rk_w_rkv[j], rk_w0[j], rk_w1[j], rk_w2[j],
                                     rk_a0[j], rk_a1[j], rk_a2[j], rk_g1[j], rk_g2[j],
                                     rk_k_k[j], rk_k_a[j], rk_r_k[j], rk_ln_w[j], rk_ln_b[j], rk_w_out[j],
                                     rk_v0[j - 1], rk_v1[j - 1], rk_v2[j - 1])
        x = x + gt1[:, None, :] * y
        h = _modulate(_rms(x, norm2_g[i]), sh2, sc2)
        x = x + gt2[:, None, :] * _swiglu(h, ffn_w_in[i], ffn_w_out[i])
    return x


_drawn_inputs = setup_inputs


def setup_inputs(seed=0):
    import zlib

    import numpy as np

    out = dict(_drawn_inputs(seed))
    spreads = {}
    factors = {'attn_q_norm': 8.0,
     'attn_k_norm': 8.0,
     'attn_sinks': 8.0,
     'rk_w1': 6.696,
     'rk_w2': 7.556,
     'rk_a0': 7.789,
     'rk_ln_w': 3.381,
     'rk_ln_b': 40.963}
    for name, (base, spread) in spreads.items():
        noise = np.random.default_rng([zlib.crc32(name.encode()), seed]).standard_normal(out[name].shape)
        drawn = base * np.exp(spread * noise) if base else spread * noise
        out[name] = jnp.asarray(drawn.astype(out[name].dtype))
    for name, factor in factors.items():
        out[name] = (out[name] * factor).astype(out[name].dtype)
    return out
```

```python
import math
from contextlib import ExitStack

import numpy as np
import concourse.bass as bass
from concourse import mybir

F32 = mybir.dt.float32
F32R = mybir.dt.float32r
I32 = mybir.dt.int32
ALU = mybir.AluOpType
ACT = mybir.ActivationFunctionType
AX = mybir.AxisListType

P = 128
D = 1024
S = 1024
KC = D // P
HALF = 512
NH = S // HALF
DEPTH = 2
HEAD = 64
QCH = 8
KCH = 2
GROUP = 4
VDIM = 256
CHUNK = 64
BAND = 3 * CHUNK
NT = S // P
FH = 2816
FSTEP = 256
FITER = FH // FSTEP
FS = FSTEP // P
PAIRS = KC
LEVELS = [1, 2, 4, 8, 16, 32]
EPS = 1e-6
GN_EPS = 64e-5
NEG = -1e30
TWO_PI = 2.0 * math.pi
PI_A = 6.28125
PI_B = float(np.float32(0.0019350051879882812))
PI_C = float(np.float32(TWO_PI - PI_A - PI_B))
ROUND = 12582912.0
ANG_MAX = 3.1415925

V_ADAB = 0
V_GAIN = V_ADAB + DEPTH * 6 * KC
V_MU = V_GAIN + 2 * DEPTH * KC
V_W0 = V_MU + 6 * KC
V_A0 = V_W0 + KC
V_KK = V_A0 + KC
V_KA = V_KK + KC
V_RK = V_KA + KC
V_LNW = V_RK + KC
V_LNB = V_LNW + KC
V_QKG = V_LNB + KC
V_C = V_QKG + QCH + KCH
V_SINK = V_C + KC
V_END = V_SINK + 16

C_IDENT = 0
C_ONES = C_IDENT + P
C_BLOCK = C_ONES + P
C_ROT = C_BLOCK + P
C_IDST = C_ROT + P
C_STRICT = C_IDST + CHUNK
C_CAUSAL = C_STRICT + CHUNK
C_BAND = C_CAUSAL + CHUNK
C_LEVEL = C_BAND + BAND
C_FREQ = C_LEVEL + len(LEVELS) * P
C_EPS = C_FREQ + 1
C_GNEPS = C_EPS + 1
C_END = C_GNEPS + 1
C_RESET = C_END
C_ALL = C_RESET + HALF


SIGNALS = """
tables*16 w_loaded0*16 w_loaded1*16 w_hi_done0 w_hi_done1 w_lo_done0 w_lo_done1 w_used0 w_used1
xin*16 slab_in0*16 slab_in1*16 slab_used0 slab_used1 cact_done mod_done mod_vec sq_done ms_step
ms_done rt_done rs_done xn_done h_done h_hi h_lo pos_in*16 ang_step red_done trig_done qk_main qk_sq
qk_aux qk_rt qk_step qk_out v_done v_out wv_in*16 wv_hi wv_lo q_staged v_staged pb_zeroed sc_done
tp_done pv_done a_step nm_done exp_done b_step p_done cur_out prev_out o_hi o_lo y_done x_done
w1_in0*16 w1_in1*16 w1_hi_done0 w1_hi_done1 w1_lo_done0 w1_lo_done1 w2_in*16 w2_hi_done w2_lo_done
w2_used up_done silu_done act_step act_done ffn_y ffn_x xx_done mix_f mix_hi mix_lo taken0 taken1
stored0*16 stored1*16 lora1_done lora1_act lora1_step lora1_lo lora2_done reset_in*16
wkv_tiles_in*16 wkv_g_in*16 wkv_kk_done wkv_t1_done wkv_l_done wkv_mx_done wkv_rn_done wkv_ar_done
wkv_bk_done wkv_bonus_done wkv_nt_done wkv_g_out wkv_sq_done_w wkv_ss_done wkv_rt_done_w wkv_e_done
wkv_eq_done wkv_bd_done wkv_tok_out wkv_ka_step wkv_k2_done wkv_lq_done wkv_kkn_done wkv_b_done
wkv_rk_step wkv_rk_done wkv_bonus_ps wkv_g1_done wkv_g2_done wkv_tok_done wkv_lev_mask wkv_x_done_w
wkv_w_done wkv_tr_done wkv_t_done wkv_xs_done wkv_xe_done wkv_us_done wkv_ue_done wkv_sn_done
wkv_s_step wkv_s_done wkv_y_done_w wkv_m_step wkv_yc_done wkv_ysq_done wkv_var_done wkv_yrt_done
wkv_yrn_done wkv_ybd_done wkv_yf_done wkv_z1_done wkv_z_step wkv_zeros chunk_used0 chunk_used1
post_done0 post_done1 z_stored*16 z_in0*16 z_in1*16 z_hi z_lo stored*16
"""


class Sig:

    def __init__(self, sem, unit=1):
        self.sem, self.unit, self.base = sem, unit, 1

    @property
    def up(self):
        return self.sem, self.unit

    def at(self, n):
        return self.sem, (self.base + n) * self.unit

    def passed(self, n):
        self.base += n


class Weights:

    def __init__(self, sb, c):
        self.raw = [sb(f"w_raw{s}", [P, KC, P], F32, c) for s in range(2)]
        self.hi = [sb(f"w_hi{s}", [P, KC, P], F32R, c) for s in range(2)]
        self.lo = [sb(f"w_lo{s}", [P, KC, P], F32R, c) for s in range(2)]


def build_program(nc, t):
    ctx = ExitStack()
    with ctx:
        stage = [0]

        def sb(name, shape, dt=F32, c=ctx):
            stage[0] += 1
            return c.enter_context(nc.sbuf_tensor(f"{name}_{stage[0]}", shape, dt))

        sems = {}

        def sig(name, unit=1):
            assert sems[name].unit == unit, name
            return sems[name]

        def settle(eng):
            eng.wait_ge(*tables.at(2))

        for line in SIGNALS.split():
            name, _, unit = line.partition("*")
            sems[name] = Sig(ctx.enter_context(nc.semaphore(name)), int(unit or 1))

        with nc.Block() as block:
            def signal_ahead(part):
                def program(eng):
                    for x in list(sems.values())[part::4]:
                        eng.sem_inc(x.sem, x.unit)
                return program

            block.sync(signal_ahead(0))
            block.vector(signal_ahead(1))
            block.scalar(signal_ahead(2))
            block.tensor(signal_ahead(3))

        ps = ctx.enter_context(nc.psum_tensor("ps", [P, 8, HALF], F32))
        xt = sb("xt", [P, KC, S])
        vec = sb("vec", [P, V_END])
        con = sb("con", [P, C_END])
        mod = sb("mod", [P, DEPTH * 6 * KC])
        gain = sb("gain", [P, 2 * DEPTH * KC])

        tables = sig("tables", 16)

        w_loaded = [sig(f"w_loaded{s}", 16) for s in range(2)]
        w_hi_done = [sig(f"w_hi_done{s}") for s in range(2)]
        w_lo_done = [sig(f"w_lo_done{s}") for s in range(2)]
        w_used = [sig(f"w_used{s}") for s in range(2)]
        slot_signals = [w_loaded, w_hi_done, w_lo_done, w_used]

        def load_weights(sp, w, s, i, src):
            sp.wait_ge(*w_lo_done[s].at(i))
            settle(sp)
            sp.dma_start(w.raw[s][:, :, :], src).then_inc(*w_loaded[s].up)

        def split_hi(act, w, s, i):
            act.wait_ge(*w_loaded[s].at(i + 1))
            act.wait_ge(*w_used[s].at(i))
            act.activation(w.hi[s][:, :, :], w.raw[s][:, :, :], ACT.Copy).then_inc(*w_hi_done[s].up)

        def split_lo(pool, w, s, i):
            pool.wait_ge(*w_hi_done[s].at(i + 1))
            pool.tensor_tensor(w.lo[s][:, :, :], w.raw[s][:, :, :],
                                               w.hi[s][:, :, :].bitcast(F32), ALU.subtract).then_inc(*w_lo_done[s].up)

        def product(pe, out, w_hi, w_lo, x_hi, x_lo, kc=KC, first=True, last=True):
            for k in range(kc):
                pe.matmul(out, w_hi(k), x_hi(k), start=first and k == 0, stop=False)
                pe.matmul(out, w_hi(k), x_lo(k), start=False, stop=False)
                ins = pe.matmul(out, w_lo(k), x_hi(k), start=False, stop=last and k == kc - 1)
            return ins

        def slots_passed(n):
            for group in slot_signals:
                for s in range(2):
                    group[s].passed(n)

        def ada_phase():
            with ExitStack() as c:
                slab = [sb(f"slab{s}", [P, KC, D], c=c) for s in range(2)]
                cact = sb("cact", [P, KC], c=c)
                tmp = sb("ada_tmp", [P, 2 * DEPTH * KC], c=c)
                xin = sig("xin", 16)
                slab_in = [sig(f"slab_in{s}", 16) for s in range(2)]
                slab_used = [sig(f"slab_used{s}") for s in range(2)]
                cact_done, mod_done, mod_vec = sig("cact_done"), sig("mod_done"), sig("mod_vec")
                with nc.Block() as block:
                    @block.sync
                    def _(sp):
                        sp.dma_start(vec[:, :], t["vecs"]).then_inc(*tables.up)
                        sp.dma_start(con[:, :], t["consts"][:, 0:C_END]).then_inc(*tables.up)
                        with sp.Fori(0, DEPTH * 3) as i:
                            for s in range(2):
                                sp.wait_ge(*slab_used[s].at(i))
                                settle(sp)
                                sp.dma_start(slab[s][:, :, :], t["ada_w"][bass.ds(2 * i + s, 1)].rearrange("a p k n -> (a p) k n")).then_inc(*slab_in[s].up)
                        sp.dma_start(xt[:, :, :], t["xT"]).then_inc(*xin.up)
                        sp.wait_ge(*xin.at(1))

                    @block.scalar
                    def _(act):
                        act.wait_ge(*tables.at(2))
                        act.activation(cact[:, :], vec[:, V_C:V_C + KC], ACT.Silu).then_inc(*cact_done.up)

                    @block.tensor
                    def _(pe):
                        pe.wait_ge(*cact_done.at(1))
                        with pe.Fori(0, DEPTH * 3) as i:
                            for s in range(2):
                                pe.wait_ge(*slab_in[s].at(i + 1))
                                for j in range(KC):
                                    for k in range(KC):
                                        ins = pe.matmul(ps[:, 0, bass.ds((2 * i + s) * KC + j, 1)],
                                                        slab[s][:, k, j * P:(j + 1) * P], cact[:, k:k + 1],
                                                        start=k == 0, stop=k == KC - 1)
                                ins.then_inc(*slab_used[s].up)

                    @block.vector
                    def _(dve):
                        for s in range(2):
                            dve.wait_ge(*slab_used[s].at(DEPTH * 3))
                        dve.tensor_tensor(mod[:, :], ps[:, 0, 0:DEPTH * 6 * KC],
                                                      vec[:, V_ADAB:V_ADAB + DEPTH * 6 * KC], ALU.add).then_inc(*mod_done.up)
                        dve.wait_ge(*mod_done.at(1))
                        for n in range(2 * DEPTH):
                            sc = (n // 2) * 6 * KC + (3 * (n % 2) + 1) * KC
                            dve.scalar_tensor_tensor(
                                gain[:, n * KC:(n + 1) * KC], mod[:, sc:sc + KC], 1.0,
                                vec[:, V_GAIN + n * KC:V_GAIN + (n + 1) * KC], ALU.add, ALU.mult).then_inc(*mod_vec.up)
                        dve.tensor_scalar(vec[:, V_QKG:V_QKG + QCH], vec[:, V_QKG:V_QKG + QCH],
                                                     HEAD ** -0.5, None, ALU.mult).then_inc(*mod_vec.up)

        def norm_phase(n, hi=None, lo=None, plain=None):
            with ExitStack() as c:
                sq = [sb(f"sq{s}", [P, S], c=c) for s in range(2)]
                rs = sb("rs", [P, S], c=c)
                xn = [sb(f"xn{s}", [P, S], c=c) for s in range(2)]
                hf = [sb(f"hf{s}", [P, S], c=c) for s in range(2)] if plain is None else None
                sq_done, ms_step, ms_done = sig("sq_done"), sig("ms_step"), sig("ms_done")
                rt_done, rs_done, xn_done = sig("rt_done"), sig("rs_done"), sig("xn_done")
                h_done, h_hi, h_lo = sig("h_done"), sig("h_hi"), sig("h_lo")
                shift = (n // 2) * 6 * KC + 3 * (n % 2) * KC
                with nc.Block() as block:
                    @block.scalar
                    def _(act):
                        for k in range(KC):
                            if k >= 2:
                                act.wait_ge(*ms_step.at(k - 1))
                            act.activation(sq[k % 2][:, :], xt[:, k, :], ACT.Square).then_inc(*sq_done.up)
                        for h in range(NH):
                            act.wait_ge(*ms_done.at(h + 1))
                            act.activation(rs[:, h * HALF:(h + 1) * HALF], ps[:, h, :], ACT.Sqrt,
                                                      scale=1.0 / D, bias=con[:, C_EPS:C_EPS + 1]).then_inc(*rt_done.up)
                        if plain is None:
                            for k in range(KC):
                                act.wait_ge(*h_done.at(k + 1))
                                act.activation(hi[:, k, :], hf[k % 2][:, :], ACT.Copy).then_inc(*h_hi.up)

                    @block.tensor
                    def _(pe):
                        for k in range(KC):
                            pe.wait_ge(*sq_done.at(k + 1))
                            for h in range(NH):
                                ins = pe.matmul(ps[:, h, :], con[:, C_ONES:C_ONES + P],
                                                sq[k % 2][:, h * HALF:(h + 1) * HALF], start=k == 0, stop=k == KC - 1)
                                if k == KC - 1:
                                    ins.then_inc(*ms_done.up)
                            if k < KC - 1:
                                ins.then_inc(*ms_step.up)

                    @block.vector
                    def _(dve):
                        for h in range(NH):
                            dve.wait_ge(*rt_done.at(h + 1))
                            dve.reciprocal(rs[:, h * HALF:(h + 1) * HALF], rs[:, h * HALF:(h + 1) * HALF]).then_inc(*rs_done.up)
                        dve.wait_ge(*rs_done.at(NH))
                        for k in range(KC):
                            if k >= 2:
                                dve.wait_ge(*h_done.at(k - 1))
                            dve.tensor_tensor(xn[k % 2][:, :], xt[:, k, :], rs[:, :], ALU.mult).then_inc(*xn_done.up)
                            dve.wait_ge(*xn_done.at(k + 1))
                            if plain is None and k >= 2:
                                dve.wait_ge(*h_lo.at(k - 1))
                            out = plain[:, k, 1:S + 1] if plain is not None else hf[k % 2][:, :]
                            dve.tensor_scalar(out, xn[k % 2][:, :], gain[:, n * KC + k:n * KC + k + 1],
                                                        mod[:, shift + k:shift + k + 1], ALU.mult, ALU.add).then_inc(*h_done.up)

                    @block.gpsimd
                    def _(pool):
                        if plain is not None:
                            pool.memset(plain[:, :, 0:1], 0.0).then_inc(*h_lo.up)
                            return
                        for k in range(KC):
                            pool.wait_ge(*h_hi.at(k + 1))
                            pool.tensor_tensor(lo[:, k, :], hf[k % 2][:, :], hi[:, k, :].bitcast(F32),
                                                       ALU.subtract).then_inc(*h_lo.up)
                sq_done.passed(KC), ms_step.passed(KC - 1), ms_done.passed(NH), rt_done.passed(NH)
                rs_done.passed(NH), xn_done.passed(KC), h_done.passed(KC)
                h_hi.passed(KC if plain is None else 0)
                h_lo.passed(KC if plain is None else 1)

        def out_phase(w, src, gate, hi, lo):
            y_done, x_done = sig("y_done"), sig("x_done")
            with nc.Block() as block:
                @block.sync
                def _(sp):
                    with sp.Fori(0, KC // 2) as i:
                        for s in range(2):
                            load_weights(sp, w, s, i, src[bass.ds(2 * i + s, 1)].rearrange("a p k n -> (a p) k n"))

                @block.scalar
                def _(act):
                    with act.Fori(0, KC // 2) as i:
                        for s in range(2):
                            split_hi(act, w, s, i)

                @block.gpsimd
                def _(pool):
                    with pool.Fori(0, KC // 2) as i:
                        for s in range(2):
                            split_lo(pool, w, s, i)

                @block.tensor
                def _(pe):
                    with pe.Fori(0, KC // 2) as i:
                        for s in range(2):
                            pe.wait_ge(*w_lo_done[s].at(i + 1))
                            pe.wait_ge(*x_done.at(4 * i))
                            for h in range(NH):
                                hs = slice(h * HALF, (h + 1) * HALF)
                                ins = product(pe, ps[:, 2 * s + h, :], lambda k: w.hi[s][:, k, :],
                                              lambda k: w.lo[s][:, k, :], lambda k: hi[:, k, hs], lambda k: lo[:, k, hs])
                                ins.then_inc(*y_done.up) if h == 0 else None
                            ins.then_inc(*w_used[s].up)

                @block.vector
                def _(dve):
                    with dve.Fori(0, KC // 2) as i:
                        for s in range(2):
                            for h in range(NH):
                                if h == 0:
                                    dve.wait_ge(*y_done.at(2 * i + s + 1))
                                else:
                                    dve.wait_ge(*w_used[s].at(i + 1))
                                xs = xt[:, bass.ds(2 * i + s, 1), h * HALF:(h + 1) * HALF].rearrange("p a n -> p (a n)")
                                dve.scalar_tensor_tensor(xs, ps[:, 2 * s + h, :],
                                                                   mod[:, bass.ds(gate + 2 * i + s, 1)],
                                                                   xs, ALU.mult, ALU.add).then_inc(*x_done.up)
            slots_passed(KC // 2)
            y_done.passed(KC), x_done.passed(2 * KC)

        def rope_phase(cos, sin):
            with ExitStack() as c:
                pos = sb("pos", [P, S], I32, c)
                ang = sb("ang", [P, S], c=c)
                turns = sb("turns", [P, S], c=c)
                red = sb("red", [P, S], c=c)
                pos_in, ang_step, red_done, trig = sig("pos_in", 16), sig("ang_step"), sig("red_done"), sig("trig_done")
                with nc.Block() as block:
                    @block.sync
                    def _(sp):
                        sp.dma_start(pos[:, :], t["positions"]).then_inc(*pos_in.up)

                    @block.vector
                    def _(dve):
                        n = [0]

                        def step(ins):
                            ins.then_inc(*ang_step.up)
                            n[0] += 1
                            dve.wait_ge(*ang_step.at(n[0]))

                        dve.wait_ge(*pos_in.at(1))
                        step(dve.tensor_copy(ang[:, :], pos[:, :]))
                        step(dve.tensor_scalar(ang[:, :], ang[:, :], con[:, C_FREQ:C_FREQ + 1], None, ALU.mult))
                        for j, quarter in enumerate((0.0, 0.25)):
                            step(dve.tensor_scalar(turns[:, :], ang[:, :], 1.0 / TWO_PI, quarter, ALU.mult, ALU.add))
                            step(dve.tensor_scalar(turns[:, :], turns[:, :], ROUND, None, ALU.add))
                            step(dve.tensor_scalar(turns[:, :], turns[:, :], ROUND, None, ALU.subtract))
                            if j == 1:
                                dve.wait_ge(*trig.at(1))
                            step(dve.scalar_tensor_tensor(red[:, :], turns[:, :], -PI_A, ang[:, :], ALU.mult, ALU.add))
                            for part in (PI_B, PI_C):
                                step(dve.scalar_tensor_tensor(red[:, :], turns[:, :], -part, red[:, :], ALU.mult, ALU.add))
                            step(dve.tensor_scalar(red[:, :], red[:, :], quarter * TWO_PI, ANG_MAX, ALU.add, ALU.min))
                            dve.tensor_scalar(red[:, :], red[:, :], -ANG_MAX, None, ALU.max).then_inc(*red_done.up)
                        n_steps[0] = n[0]

                    @block.scalar
                    def _(act):
                        for j, out in enumerate((sin, cos)):
                            act.wait_ge(*red_done.at(j + 1))
                            act.activation(out[:, :], red[:, :], ACT.Sin).then_inc(*trig.up)
                pos_in.passed(1), ang_step.passed(n_steps[0]), red_done.passed(2), trig.passed(2)

        n_steps = [0]

        def qkv_phase(w, hi, lo, cos, sin, qk, vt):
            NQ = QCH + KCH
            with ExitStack() as c:
                raw = [sb(f"qk_raw{h}", [P, HALF], c=c) for h in range(NH)]
                sq = [sb(f"qk_sq{h}", [P, HALF], c=c) for h in range(NH)]
                rt = [sb(f"qk_rt{h}", [P, HALF], c=c) for h in range(NH)]
                m1 = [sb(f"qk_m1{h}", [P, HALF], c=c) for h in range(NH)]
                m2 = [sb(f"qk_m2{h}", [P, HALF], c=c) for h in range(NH)]
                main_done, sq_done, aux_done = sig("qk_main"), sig("qk_sq"), sig("qk_aux")
                rt_done, step_done, out_done = sig("qk_rt"), sig("qk_step"), sig("qk_out")
                v_done, v_out = sig("v_done"), sig("v_out")
                wv_in, wv_hi, wv_lo = sig("wv_in", 16), sig("wv_hi"), sig("wv_lo")
                with nc.Block() as block:
                    @block.sync
                    def _(sp):
                        with sp.Fori(0, NQ // 2) as i:
                            for s in range(2):
                                load_weights(sp, w, s, i, t["wqk"][bass.ds(2 * i + s, 1)].rearrange("a p k n -> (a p) k n"))
                        for s in range(2):
                            load_weights(sp, w, s, NQ // 2, t["wv"][s])

                    @block.scalar
                    def _(act):
                        with act.Fori(0, NQ // 2) as i:
                            for s in range(2):
                                split_hi(act, w, s, i)
                            for u in range(4):
                                s, h = divmod(u, 2)
                                if h == 0:
                                    act.wait_ge(*main_done.at(2 * i + s + 1))
                                else:
                                    act.wait_ge(*w_used[s].at(i + 1))
                                act.wait_ge(*aux_done.at(4 * i + u - 1 if u >= 2 else 4 * i))
                                act.wait_ge(*out_done.at(4 * i + u - 1 if u >= 2 else 4 * i))
                                act.activation(sq[h][:, :], ps[:, u, :], ACT.Square)
                                act.activation(raw[h][:, :], ps[:, u, :], ACT.Copy,
                                                          scale=vec[:, bass.ds(V_QKG + 2 * i + s, 1)]).then_inc(*sq_done.up)
                                for v in ([u - 1] if u in (1, 2) else [2, 3] if u == 3 else []):
                                    act.wait_ge(*aux_done.at(4 * i + v + 1))
                                    act.activation(rt[v % 2][:, :], ps[:, 4 + v % 2, :], ACT.Sqrt,
                                                              scale=1.0 / HEAD, bias=con[:, C_EPS:C_EPS + 1]).then_inc(*rt_done.up)
                        for s in range(2):
                            split_hi(act, w, s, NQ // 2)

                    @block.gpsimd
                    def _(pool):
                        with pool.Fori(0, NQ // 2) as i:
                            for s in range(2):
                                split_lo(pool, w, s, i)
                        for s in range(2):
                            split_lo(pool, w, s, NQ // 2)

                    @block.tensor
                    def _(pe):
                        def aux(i, u):
                            h = u % 2
                            pe.wait_ge(*sq_done.at(4 * i + u + 1))
                            pe.wait_ge(*out_done.at(4 * i + u - 1 if u >= 2 else 4 * i))
                            pe.matmul(ps[:, 4 + h, :], con[:, C_BLOCK:C_BLOCK + P], sq[h][:, :], start=True, stop=True)
                            pe.matmul(ps[:, 6 + h, :], con[:, C_ROT:C_ROT + P], raw[h][:, :],
                                                  start=True, stop=True).then_inc(*aux_done.up)

                        with pe.Fori(0, NQ // 2) as i:
                            pe.wait_ge(*sq_done.at(4 * i))
                            for u in range(4):
                                s, h = divmod(u, 2)
                                if h == 0:
                                    pe.wait_ge(*w_lo_done[s].at(i + 1))
                                hs = slice(h * HALF, (h + 1) * HALF)
                                ins = product(pe, ps[:, u, :], lambda k: w.hi[s][:, k, :], lambda k: w.lo[s][:, k, :],
                                              lambda k: hi[:, k, hs], lambda k: lo[:, k, hs])
                                ins.then_inc(*(main_done if h == 0 else w_used[s]).up)
                                if u >= 1:
                                    aux(i, u - 1)
                            aux(i, 3)
                        pe.wait_ge(*sq_done.at(4 * (NQ // 2)))
                        for s in range(2):
                            pe.wait_ge(*w_lo_done[s].at(NQ // 2 + 1))
                            for b in range(2):
                                for q in range(NT // 2):
                                    tok = slice((b * 4 + q) * P, (b * 4 + q + 1) * P)
                                    ins = product(pe, ps[:, 2 * s + b, q * P:(q + 1) * P],
                                                  lambda k: hi[:, k, tok], lambda k: lo[:, k, tok],
                                                  lambda k: w.hi[s][:, k, :], lambda k: w.lo[s][:, k, :])
                                ins.then_inc(*v_done.up) if b == 0 else ins.then_inc(*w_used[s].up)

                    @block.vector
                    def _(dve):
                        with dve.Fori(0, NQ // 2) as i:
                            for u in range(4):
                                s, h = divmod(u, 2)
                                hs = slice(h * HALF, (h + 1) * HALF)
                                dve.wait_ge(*rt_done.at(4 * i + u + 1))
                                dve.reciprocal(rt[h][:, :], rt[h][:, :]).then_inc(*step_done.up)
                                dve.tensor_tensor(m1[h][:, :], raw[h][:, :], cos[:, hs], ALU.mult).then_inc(*step_done.up)
                                dve.tensor_tensor(m2[h][:, :], ps[:, 6 + h, :], sin[:, hs], ALU.mult).then_inc(*step_done.up)
                                dve.wait_ge(*step_done.at(16 * i + 4 * u + 3))
                                dve.tensor_tensor(m1[h][:, :], m1[h][:, :], m2[h][:, :], ALU.add).then_inc(*step_done.up)
                                dve.wait_ge(*step_done.at(16 * i + 4 * u + 4))
                                out = qk[:, bass.ds(2 * i + s, 1), hs].rearrange("p a n -> p (a n)")
                                dve.tensor_tensor(out, m1[h][:, :], rt[h][:, :], ALU.mult).then_inc(*out_done.up)
                        for s in range(2):
                            for b in range(2):
                                dve.wait_ge(*v_done.at(s + 1)) if b == 0 else dve.wait_ge(*w_used[s].at(NQ // 2 + 1))
                                dve.tensor_copy(vt[:, b * 4:b * 4 + 4, s * P:(s + 1) * P],
                                                         ps[:, 2 * s + b, :].rearrange("p (q n) -> p q n", q=4)).then_inc(*v_out.up)
                slots_passed(NQ // 2 + 1)
                n = 2 * NQ
                main_done.passed(NQ), sq_done.passed(n), aux_done.passed(n), rt_done.passed(n)
                step_done.passed(4 * n), out_done.passed(n), v_done.passed(2), v_out.passed(4)

        def attention_phase(qk, vt, hi, lo):
            with ExitStack() as c:
                qs = sb("qs", [P, QCH, P], c=c)
                ks = sb("ks", [P, KCH, BAND], c=c)
                vs = sb("vs", [P, 2, VDIM], c=c)
                sc = [sb(f"sc{b}", [P, GROUP, BAND], c=c) for b in range(2)]
                pb = [sb(f"pb{b}", [P, GROUP, 2 * P], c=c) for b in range(2)]
                pt = [sb(f"pt{b}", [P, GROUP * P], c=c) for b in range(2)]
                mx = sb("mx", [P, 4, GROUP], c=c)
                nm = sb("nm", [P, 4, GROUP], c=c)
                es = sb("es", [P, 4, GROUP], c=c)
                den = sb("den", [P, 4, GROUP], c=c)
                q_staged, v_staged, zeroed = sig("q_staged"), sig("v_staged"), sig("pb_zeroed")
                sc_done, tp_done, pv_done = sig("sc_done"), sig("tp_done"), sig("pv_done")
                a_step, nm_done, exp_done, b_step = sig("a_step"), sig("nm_done"), sig("exp_done"), sig("b_step")
                p_done, cur_out, prev_out, o_hi, o_lo = (sig("p_done"), sig("cur_out"), sig("prev_out"),
                                                         sig("o_hi"), sig("o_lo"))

                def tile_loop(eng, body):
                    body(0, True)
                    with eng.Fori(1, NT) as p:
                        body(p, False)

                def span(first):
                    return slice(CHUNK, BAND) if first else slice(0, BAND)

                with nc.Block() as block:
                    @block.gpsimd
                    def _(pool):
                        for b in range(2):
                            pool.memset(pb[b][:, :, 0:CHUNK], 0.0).then_inc(*zeroed.up)

                        def body(p, first):
                            if not first:
                                pool.wait_ge(*sc_done.at(4 * p))
                            pool.tensor_copy(qs[:, :, :], qk[:, 0:QCH, bass.ds(p * P, P)])
                            if first:
                                pool.tensor_copy(ks[:, :, CHUNK:BAND], qk[:, QCH:QCH + KCH, 0:P]).then_inc(*q_staged.up)
                            else:
                                pool.tensor_copy(ks[:, :, :], qk[:, QCH:QCH + KCH, bass.ds(p * P - CHUNK, BAND)]).then_inc(*q_staged.up)
                                pool.wait_ge(*pv_done.at(4 * p))
                            if first:
                                pool.tensor_copy(vs[:, 1, :], vt[:, 0, :]).then_inc(*v_staged.up)
                            else:
                                pool.tensor_copy(vs[:, :, :], vt[:, bass.ds(p - 1, 2), :]).then_inc(*v_staged.up)

                        tile_loop(pool, body)

                    @block.tensor
                    def _(pe):
                        def body(p, first):
                            def scores(g):
                                a, s = divmod(g, 2)
                                half = slice(s * HEAD, (s + 1) * HEAD)
                                if g >= 2 or not first:
                                    pe.wait_ge(*nm_done.at(4 * p + g - 1 if g >= 2 else 4 * p))
                                for j in range(GROUP):
                                    off = (j % 2) * BAND
                                    ins = pe.matmul(ps[:, 2 * s + j // 2, off + span(first).start:off + BAND],
                                                    qs[half, a * GROUP + j, :], ks[half, a, span(first)],
                                                    start=True, stop=True)
                                ins.then_inc(*sc_done.up)

                            pe.wait_ge(*q_staged.at(p + 1))
                            scores(0), scores(1)
                            for g in range(4):
                                a, s = divmod(g, 2)
                                pe.wait_ge(*p_done.at(4 * p + g + 1))
                                if g or not first:
                                    pe.wait_ge(*cur_out.at(4 * p + g))
                                if not first:
                                    pe.wait_ge(*prev_out.at(4 * (p - 1) + g))
                                for half in ((1,) if first else (0, 1)):
                                    for j in range(GROUP):
                                        ins = pe.transpose(ps[:, 4 + half, j * P:(j + 1) * P],
                                                           pb[g % 2][:, j, half * P:(half + 1) * P],
                                                           con[:, C_IDENT:C_IDENT + P])
                                ins.then_inc(*tp_done.up)
                                if g < 2:
                                    scores(g + 2)
                                if g == 0:
                                    pe.wait_ge(*v_staged.at(p + 1))
                                if s == 0 and not first:
                                    pe.wait_ge(*o_lo.at(2 * p))
                                pe.wait_ge(*cur_out.at(4 * p + g + 1))
                                if not first:
                                    pe.wait_ge(*prev_out.at(4 * (p - 1) + g + 1))
                                for half in ((1,) if first else (0, 1)):
                                    kv = (2 * a + s) * HEAD
                                    ins = pe.matmul(ps[s * HEAD:(s + 1) * HEAD, 6 + a, :],
                                                    vs[:, half, kv:kv + HEAD], pt[half][:, :],
                                                    start=half == 1 if first else half == 0, stop=half == 1)
                                ins.then_inc(*pv_done.up)

                        tile_loop(pe, body)

                    @block.vector
                    def _(dve):
                        def body(p, first):
                            mask = con[:, C_BAND + span(first).start:C_BAND + BAND]
                            n = BAND - span(first).start

                            def maximum(g):
                                s = g % 2
                                dve.wait_ge(*sc_done.at(4 * p + g + 1))
                                if g >= 2 or not first:
                                    dve.wait_ge(*exp_done.at(4 * p + g - 1 if g >= 2 else 4 * p))
                                for b in range(2):
                                    src = ps[:, 2 * s + b, 0:2 * BAND].rearrange("p (j n) -> p j n", j=2)[:, :, span(first)]
                                    dve.tensor_tensor(sc[s][:, 2 * b:2 * b + 2, span(first)], src,
                                                                mask.unsqueeze(1).to_broadcast([P, 2, n]), ALU.add).then_inc(*a_step.up)
                                dve.wait_ge(*a_step.at(16 * p + 4 * g + 2))
                                dve.tensor_reduce(mx[:, g, :], sc[s][:, :, span(first)], AX.X, ALU.max).then_inc(*a_step.up)
                                dve.wait_ge(*a_step.at(16 * p + 4 * g + 3))
                                sink = vec[:, V_SINK + 4 * g:V_SINK + 4 * g + 4]
                                dve.tensor_tensor(mx[:, g, :], mx[:, g, :], sink, ALU.max).then_inc(*a_step.up)
                                dve.wait_ge(*a_step.at(16 * p + 4 * g + 4))
                                dve.tensor_tensor(es[:, g, :], sink, mx[:, g, :], ALU.subtract)
                                dve.tensor_scalar(nm[:, g, :], mx[:, g, :], -1.0, None, ALU.mult).then_inc(*nm_done.up)

                            def normalise(g):
                                dve.wait_ge(*exp_done.at(4 * p + g + 1))
                                dve.tensor_tensor(den[:, g, :], den[:, g, :], es[:, g, :], ALU.add).then_inc(*b_step.up)
                                dve.wait_ge(*b_step.at(8 * p + 2 * g + 1))
                                dve.reciprocal(den[:, g, :], den[:, g, :]).then_inc(*b_step.up)
                                dve.wait_ge(*b_step.at(8 * p + 2 * g + 2))
                                pv = pb[g % 2][:, :, CHUNK + span(first).start:2 * P]
                                dve.tensor_tensor(pv, pv, den[:, g, :].unsqueeze(2).to_broadcast([P, GROUP, n]),
                                                            ALU.mult).then_inc(*p_done.up)

                            def take_current(g):
                                dve.wait_ge(*tp_done.at(4 * p + g + 1))
                                if g or not first:
                                    dve.wait_ge(*pv_done.at(4 * p + g))
                                dve.tensor_copy(pt[1][:, :], ps[:, 5, :]).then_inc(*cur_out.up)

                            def low_part(a):
                                dve.wait_ge(*o_hi.at(2 * p + a + 1))
                                tok = bass.ds(p * P, P)
                                dve.tensor_tensor(lo[:, a * GROUP:(a + 1) * GROUP, tok],
                                                          ps[:, 6 + a, :].rearrange("p (j n) -> p j n", j=GROUP),
                                                          hi[:, a * GROUP:(a + 1) * GROUP, tok].bitcast(F32), ALU.subtract).then_inc(*o_lo.up)

                            maximum(0), maximum(1), normalise(0)
                            take_current(0), maximum(2), normalise(1)
                            take_current(1), maximum(3), normalise(2)
                            take_current(2), low_part(0), normalise(3)
                            take_current(3), low_part(1)

                        tile_loop(dve, body)

                    @block.scalar
                    def _(act):
                        def body(p, first):
                            if first:
                                act.wait_ge(*zeroed.at(2))

                            def exponentials(g):
                                act.wait_ge(*nm_done.at(4 * p + g + 1))
                                if g >= 2 or not first:
                                    act.wait_ge(*tp_done.at(4 * p + g - 1 if g >= 2 else 4 * p))
                                for j in range(GROUP):
                                    act.activation(pb[g % 2][:, j, CHUNK + span(first).start:2 * P], sc[g % 2][:, j, span(first)],
                                                   ACT.Exp, bias=nm[:, g, j:j + 1],
                                                   accum_out=den[:, g, j:j + 1])
                                act.activation(es[:, g, :], es[:, g, :], ACT.Exp).then_inc(*exp_done.up)

                            def take_previous(g):
                                if first:
                                    return
                                act.wait_ge(*tp_done.at(4 * p + g + 1))
                                act.wait_ge(*pv_done.at(4 * p + g))
                                act.activation(pt[0][:, :], ps[:, 4, :], ACT.Copy).then_inc(*prev_out.up)

                            def high_part(a):
                                act.wait_ge(*pv_done.at(4 * p + 2 * a + 2))
                                settle(act)
                                act.activation(hi[:, a * GROUP:(a + 1) * GROUP, bass.ds(p * P, P)],
                                                       ps[:, 6 + a, :].rearrange("p (j n) -> p j n", j=GROUP), ACT.Copy).then_inc(*o_hi.up)

                            exponentials(0), exponentials(1)
                            take_previous(0), exponentials(2)
                            take_previous(1), exponentials(3)
                            take_previous(2), high_part(0)
                            take_previous(3), high_part(1)

                        tile_loop(act, body)
                q_staged.passed(NT), v_staged.passed(NT), zeroed.passed(2)
                for x in (sc_done, tp_done, pv_done, nm_done, exp_done, p_done, cur_out):
                    x.passed(4 * NT)
                prev_out.passed(4 * (NT - 1))
                a_step.passed(16 * NT), b_step.passed(8 * NT), o_hi.passed(2 * NT), o_lo.passed(2 * NT)

        def ffn_phase(layer, hi, lo):
            with ExitStack() as c:
                w1 = [sb(f"w1_raw{f}", [P, KC, 2 * P], c=c) for f in range(FS)]
                w1h = [sb(f"w1_hi{f}", [P, KC, 2 * P], F32R, c) for f in range(FS)]
                w1l = [sb(f"w1_lo{f}", [P, KC, 2 * P], F32R, c) for f in range(FS)]
                w2 = sb("w2_raw", [P, FS, D], c=c)
                w2h, w2l = sb("w2_hi", [P, FS, D], F32R, c), sb("w2_lo", [P, FS, D], F32R, c)
                ah, al = sb("act_hi", [P, FS, S], F32R, c), sb("act_lo", [P, FS, S], F32R, c)
                sg = [sb(f"silu{b}", [P, HALF], c=c) for b in range(2)]
                af = [sb(f"act{b}", [P, HALF], c=c) for b in range(2)]
                w1_in = [sig(f"w1_in{f}", 16) for f in range(FS)]
                w1_hi = [sig(f"w1_hi_done{f}") for f in range(FS)]
                w1_lo = [sig(f"w1_lo_done{f}") for f in range(FS)]
                w2_in, w2_hi, w2_lo, w2_used = sig("w2_in", 16), sig("w2_hi_done"), sig("w2_lo_done"), sig("w2_used")
                up_done, silu_done, act_step, act_done = sig("up_done"), sig("silu_done"), sig("act_step"), sig("act_done")
                y_done, x_done = sig("ffn_y"), sig("ffn_x")
                win, wout = t["ffn_w_in"], t["ffn_w_out"]

                with nc.Block() as block:
                    @block.sync
                    def _(sp):
                        def load_in(i, f):
                            sp.wait_ge(*w1_lo[f].at(i))
                            settle(sp)
                            sp.dma_start(w1[f][:, :, :], win[bass.ds((layer * FITER + i) * FS + f, 1)]
                                                     .rearrange("a p k n -> (a p) k n")).then_inc(*w1_in[f].up)

                        def load_out(i):
                            sp.wait_ge(*w2_lo.at(i))
                            settle(sp)
                            sp.dma_start(w2[:, :, :], wout[bass.ds(layer * FITER + i, 1)]
                                                  .rearrange("a p f n -> (a p) f n")).then_inc(*w2_in.up)

                        with sp.Fori(0, FITER) as i:
                            load_in(i, 0), load_in(i, 1), load_out(i)

                    def split_in_hi(act, i, f, prior=None):
                        act.wait_ge(*w1_in[f].at(i + 1))
                        if prior is not None:
                            act.wait_ge(*up_done.at(prior))
                        act.activation(w1h[f][:, :, :], w1[f][:, :, :], ACT.Copy).then_inc(*w1_hi[f].up)

                    def split_in_lo(pool, i, f):
                        pool.wait_ge(*w1_hi[f].at(i + 1))
                        pool.tensor_tensor(w1l[f][:, :, :], w1[f][:, :, :], w1h[f][:, :, :].bitcast(F32),
                                                       ALU.subtract).then_inc(*w1_lo[f].up)

                    @block.scalar
                    def _(act):
                        def silu(i, q):
                            act.wait_ge(*up_done.at(4 * i + q + 1))
                            act.wait_ge(*act_done.at(4 * i + q - 1 if q >= 2 else 4 * i))
                            act.activation(sg[q % 2][:, :], ps[:, 2 * (q % 2), :], ACT.Silu).then_inc(*silu_done.up)

                        def step(i, last):
                            silu(i, 0)
                            act.wait_ge(*w2_in.at(i + 1))
                            act.wait_ge(*w2_used.at(i))
                            act.activation(w2h[:, :, :], w2[:, :, :], ACT.Copy).then_inc(*w2_hi.up)
                            silu(i, 1), silu(i, 2)
                            if not last:
                                split_in_hi(act, i + 1, 0, 4 * i + 3)
                            silu(i, 3)
                            if not last:
                                split_in_hi(act, i + 1, 1, 4 * i + 4)

                        split_in_hi(act, 0, 0), split_in_hi(act, 0, 1)
                        with act.Fori(0, FITER - 1) as i:
                            step(i, False)
                        step(FITER - 1, True)

                    @block.gpsimd
                    def _(pool):
                        def out_lo(i):
                            pool.wait_ge(*w2_hi.at(i + 1))
                            pool.tensor_tensor(w2l[:, :, :], w2[:, :, :], w2h[:, :, :].bitcast(F32), ALU.subtract).then_inc(*w2_lo.up)

                        split_in_lo(pool, 0, 0), split_in_lo(pool, 0, 1)
                        with pool.Fori(0, FITER - 1) as i:
                            out_lo(i), split_in_lo(pool, i + 1, 0), split_in_lo(pool, i + 1, 1)
                        out_lo(FITER - 1)

                    @block.tensor
                    def _(pe):
                        with pe.Fori(0, FITER) as i:
                            for q in range(4):
                                h, f = divmod(q, 2)
                                hs = slice(h * HALF, (h + 1) * HALF)
                                if h == 0:
                                    pe.wait_ge(*w1_lo[f].at(i + 1))
                                pe.wait_ge(*act_done.at(4 * i + q - 1 if q >= 2 else 4 * i))
                                for g in range(2):
                                    gs = slice(g * P, (g + 1) * P)
                                    ins = product(pe, ps[:, 2 * f + g, :], lambda k: w1h[f][:, k, gs],
                                                  lambda k: w1l[f][:, k, gs], lambda k: hi[:, k, hs], lambda k: lo[:, k, hs])
                                ins.then_inc(*up_done.up)
                            for r in range(2 * KC):
                                h, d = divmod(r, KC)
                                hs = slice(h * HALF, (h + 1) * HALF)
                                ds = slice(d * P, (d + 1) * P)
                                if r == 0:
                                    pe.wait_ge(*w2_lo.at(i + 1))
                                if d == 0:
                                    pe.wait_ge(*act_done.at(4 * i + 2 * h + 2))
                                pe.wait_ge(*x_done.at(16 * i + r - 3 if r >= 4 else 16 * i))
                                ins = product(pe, ps[:, 4 + r % 4, :], lambda k: w2h[:, k, ds], lambda k: w2l[:, k, ds],
                                              lambda k: ah[:, k, hs], lambda k: al[:, k, hs], kc=FS)
                                ins.then_inc(*(y_done if r < 2 * KC - 1 else w2_used).up)

                    @block.vector
                    def _(dve):
                        with dve.Fori(0, FITER) as i:
                            for q in range(4):
                                h, f = divmod(q, 2)
                                hs = slice(h * HALF, (h + 1) * HALF)
                                dve.wait_ge(*silu_done.at(4 * i + q + 1))
                                dve.tensor_tensor(af[f][:, :], ps[:, 2 * f + 1, :], sg[f][:, :], ALU.mult).then_inc(*act_step.up)
                                dve.wait_ge(*act_step.at(8 * i + 2 * q + 1))
                                dve.tensor_copy(ah[:, f, hs], af[f][:, :]).then_inc(*act_step.up)
                                dve.wait_ge(*act_step.at(8 * i + 2 * q + 2))
                                dve.tensor_tensor(al[:, f, hs], af[f][:, :], ah[:, f, hs].bitcast(F32),
                                                              ALU.subtract).then_inc(*act_done.up)
                            for r in range(2 * KC):
                                h, d = divmod(r, KC)
                                xs = xt[:, d, h * HALF:(h + 1) * HALF]
                                if r < 2 * KC - 1:
                                    dve.wait_ge(*y_done.at((2 * KC - 1) * i + r + 1))
                                else:
                                    dve.wait_ge(*w2_used.at(i + 1))
                                g = (layer * 6 + 5) * KC + d
                                dve.scalar_tensor_tensor(xs, ps[:, 4 + r % 4, :], mod[:, g:g + 1], xs,
                                                                   ALU.mult, ALU.add).then_inc(*x_done.up)
                for f in range(FS):
                    for x in (w1_in, w1_hi, w1_lo):
                        x[f].passed(FITER)
                for x in (w2_in, w2_hi, w2_lo, w2_used):
                    x.passed(FITER)
                for x in (up_done, silu_done, act_done):
                    x.passed(4 * FITER)
                act_step.passed(8 * FITER), y_done.passed((2 * KC - 1) * FITER), x_done.passed(2 * KC * FITER)

        def rwkv_projections():
            scr = t["scratch"]
            with ExitStack() as c:
                h = sb("h_prev", [P, KC, S + 1], c=c)
                norm_phase(2, plain=h)
                w = Weights(sb, c)
                xx = sb("xx", [P, KC, S], c=c)
                mh = [sb(f"mix_hi{b}", [P, KC, HALF], F32R, c) for b in range(NH)]
                ml = [sb(f"mix_lo{b}", [P, KC, HALF], F32R, c) for b in range(NH)]
                with ExitStack() as c2:
                    mf = [sb(f"mix{b}", [P, HALF], c=c2) for b in range(2)]
                    stage = [sb(f"stage{b}", [P, HALF], c=c2) for b in range(2)]
                    tf, th, tl = sb("lora", [P, HALF], c=c2), sb("lora_hi", [P, HALF], F32R, c2), sb("lora_lo", [P, HALF], F32R, c2)
                    xx_done, mix_f, mix_h, mix_l = sig("xx_done"), sig("mix_f"), sig("mix_hi"), sig("mix_lo")
                    taken = [sig(f"taken{s}") for s in range(2)]
                    stored = [sig(f"stored{s}", 16) for s in range(2)]
                    lo1_done, lo1_act, lo1_step, lo1_lo = sig("lora1_done"), sig("lora1_act"), sig("lora1_step"), sig("lora1_lo")
                    lo2_done = sig("lora2_done")
                    NCH = 2 * 3 * KC // 2

                    def scratch_of(a, half, j):
                        return scr[a, half * 8:(half + 1) * 8, :, j, :].rearrange("c p n -> p c n")

                    def mix_make(dve, n, half, mix, k):
                        m = KC * n + k
                        if isinstance(m, int) and m < 2:
                            pass
                        else:
                            dve.wait_ge(*mix_l.at(m - 1))
                        hs = slice(half * HALF, (half + 1) * HALF)
                        kk = k if isinstance(k, int) else None
                        ks = slice(k, k + 1) if kk is not None else bass.ds(k, 1)
                        dve.scalar_tensor_tensor(
                            mf_of(k)[:, :], xx[:, ks, hs].rearrange("p a n -> p (a n)"),
                            vec[:, bass.ds(V_MU + mix * KC + k, 1)],
                            h[:, ks, half * HALF + 1:(half + 1) * HALF + 1].rearrange("p a n -> p (a n)"), ALU.mult, ALU.add).then_inc(*mix_f.up)

                    slot = [0]

                    def mf_of(k):
                        return mf[k % 2] if isinstance(k, int) else mf[slot[0]]

                    def one(buf, k):
                        return buf[:, bass.ds(k, 1), :].rearrange("p a n -> p (a n)")

                    def mix_high(act, n, half, k):
                        act.wait_ge(*mix_f.at(KC * n + k + 1))
                        settle(act)
                        act.activation(one(mh[half], k), mf_of(k)[:, :], ACT.Copy).then_inc(*mix_h.up)

                    def mix_low(pool, n, half, k):
                        pool.wait_ge(*mix_h.at(KC * n + k + 1))
                        pool.tensor_tensor(one(ml[half], k), mf_of(k)[:, :], one(mh[half], k).bitcast(F32),
                                                    ALU.subtract).then_inc(*mix_l.up)

                    def rkv_loop(eng, body):
                        with eng.Fori(0, 3) as p:
                            for half in range(NH):
                                with eng.Fori(0, KC // 2) as cc:
                                    for s in range(2):
                                        slot[0] = s
                                        body(p, half, cc, s, 4 * (2 * p + half) + cc, 2 * p + half)

                    with nc.Block() as block:
                        @block.sync
                        def _(sp):
                            rkv_loop(sp, lambda p, half, cc, s, i, n: load_weights(
                                sp, w, s, i, t["w_rkv"][bass.ds(p * KC + 2 * cc + s, 1)].rearrange("a p k n -> (a p) k n")))
                            for l in range(3):
                                load_weights(sp, w, 0, NCH + l, t["lora1"][l])
                                load_weights(sp, w, 1, NCH + l, t["lora2"][l])

                        def split_hi_dve(dve, s, i):
                            dve.wait_ge(*w_loaded[s].at(i + 1))
                            dve.wait_ge(*w_used[s].at(i))
                            dve.tensor_copy(w.hi[s][:, :, :], w.raw[s][:, :, :]).then_inc(*w_hi_done[s].up)

                        @block.vector
                        def _(dve):
                            for k in range(KC):
                                dve.tensor_tensor(xx[:, k, :], h[:, k, 0:S], h[:, k, 1:S + 1], ALU.subtract).then_inc(*xx_done.up)
                            dve.wait_ge(*xx_done.at(KC))
                            for k in range(KC):
                                mix_make(dve, 0, 0, 0, k)

                            def body(p, half, cc, s, i, n):
                                split_hi_dve(dve, s, i)
                                mix_make(dve, n + 1, 1 - half, p + half, 2 * cc + s)
                            rkv_loop(dve, body)
                            for l in range(3):
                                split_hi_dve(dve, 0, NCH + l)
                                split_hi_dve(dve, 1, NCH + l)
                                for half in range(NH):
                                    n = 6 + 2 * l + half
                                    if n < 11:
                                        for k in range(KC):
                                            mix_make(dve, n + 1, 1 - half, 3 + l + half, k)
                                    dve.wait_ge(*lo1_act.at(n - 5))
                                    dve.tensor_copy(th[:, :], tf[:, :]).then_inc(*lo1_step.up)
                                    dve.wait_ge(*lo1_step.at(n - 5))
                                    dve.tensor_tensor(tl[:, :], tf[:, :], th[:, :].bitcast(F32), ALU.subtract).then_inc(*lo1_lo.up)

                        @block.gpsimd
                        def _(pool):
                            for k in range(KC):
                                mix_low(pool, 0, 0, k)

                            def body(p, half, cc, s, i, n):
                                split_lo(pool, w, s, i)
                                mix_low(pool, n + 1, 1 - half, 2 * cc + s)
                            rkv_loop(pool, body)
                            for l in range(3):
                                split_lo(pool, w, 0, NCH + l)
                                split_lo(pool, w, 1, NCH + l)
                                for half in range(NH):
                                    n = 6 + 2 * l + half
                                    if n < 11:
                                        for k in range(KC):
                                            mix_low(pool, n + 1, 1 - half, k)

                        @block.scalar
                        def _(act):
                            for k in range(KC):
                                mix_high(act, 0, 0, k)

                            def take(src, s, i, func, bias, dst):
                                act.wait_ge(*stored[s].at(i))
                                act.activation(stage[s][:, :], src, func, bias=bias).then_inc(*taken[s].up)
                                act.wait_ge(*taken[s].at(i + 1))
                                settle(act)
                                act.dma_start(dst, stage[s][:, :].rearrange("p (c n) -> p c n", n=CHUNK)).then_inc(*stored[s].up)

                            def body(p, half, cc, s, i, n):
                                act.wait_ge(*w_used[1].at(4 * n))
                                mix_high(act, n + 1, 1 - half, 2 * cc + s)
                                act.wait_ge(*w_used[s].at(i + 1))
                                dst = scr[bass.ds(p, 1), half * 8:(half + 1) * 8, :, bass.ds(2 * cc + s, 1), :]
                                take(ps[:, s, :], s, i, ACT.Copy, 0.0, dst.rearrange("b c p a n -> p (b c) (a n)"))
                            rkv_loop(act, body)
                            act.wait_ge(*w_used[1].at(NCH))
                            for l, func in enumerate((ACT.Tanh, ACT.Copy, ACT.Sigmoid)):
                                for half in range(NH):
                                    n = 6 + 2 * l + half
                                    act.wait_ge(*lo1_done.at(n - 5))
                                    if n > 6:
                                        act.wait_ge(*lo2_done.at((n - 6) * KC))
                                    act.activation(tf[:, :], ps[:, 2 + half, :], func).then_inc(*lo1_act.up)
                                    if n < 11:
                                        for k in range(KC):
                                            mix_high(act, n + 1, 1 - half, k)
                                    for j in range(KC):
                                        act.wait_ge(*lo2_done.at((n - 6) * KC + j + 1))
                                        col = (V_W0, V_A0, None)[l]
                                        take(ps[:, 4 + j % 2, :], j % 2, NCH + (n - 6) * 4 + j // 2,
                                             ACT.Sigmoid if l < 2 else ACT.Copy,
                                             vec[:, col + j:col + j + 1] if l < 2 else 0.0, scratch_of(3 + l, half, j))
                            for s in range(2):
                                act.wait_ge(*stored[s].at(NCH + 24))

                        @block.tensor
                        def _(pe):
                            def body(p, half, cc, s, i, n):
                                pe.wait_ge(*w_lo_done[s].at(i + 1))
                                pe.wait_ge(*mix_l.at(KC * n + KC))
                                pe.wait_ge(*taken[s].at(i))
                                product(pe, ps[:, s, :], lambda k: w.hi[s][:, k, :], lambda k: w.lo[s][:, k, :],
                                                     lambda k: mh[half][:, k, :], lambda k: ml[half][:, k, :]).then_inc(*w_used[s].up)
                            rkv_loop(pe, body)
                            for l in range(3):
                                pe.wait_ge(*w_lo_done[0].at(NCH + l + 1))
                                pe.wait_ge(*w_lo_done[1].at(NCH + l + 1))
                                for half in range(NH):
                                    n = 6 + 2 * l + half
                                    pe.wait_ge(*mix_l.at(KC * n + KC))
                                    if n > 7:
                                        pe.wait_ge(*lo1_act.at(n - 7))
                                    product(pe, ps[:, 2 + half, :], lambda k: w.hi[0][:, k, :],
                                                        lambda k: w.lo[0][:, k, :], lambda k: mh[half][:, k, :],
                                                        lambda k: ml[half][:, k, :]).then_inc(*lo1_done.up)
                                    pe.wait_ge(*lo1_lo.at(n - 5))
                                    for j in range(KC):
                                        if n > 6 or j >= 2:
                                            pe.wait_ge(*taken[j % 2].at(NCH + (n - 6) * 4 + j // 2))
                                        product(pe, ps[:, 4 + j % 2, :], lambda k: w.hi[1][:, j, :],
                                                            lambda k: w.lo[1][:, j, :], lambda k: th[:, :],
                                                            lambda k: tl[:, :], kc=1).then_inc(*lo2_done.up)
                                for s in range(2):
                                    pe.matmul(ps[:, 6, 0:1], con[:, C_IDENT:C_IDENT + P], con[:, 0:1],
                                                           start=True, stop=True).then_inc(*w_used[s].up)
                    slots_passed(NCH + 3)
                    xx_done.passed(KC), mix_f.passed(12 * KC), mix_h.passed(12 * KC), mix_l.passed(12 * KC)
                    for s in range(2):
                        taken[s].passed(NCH + 24), stored[s].passed(NCH + 24)
                    for x in (lo1_done, lo1_act, lo1_step, lo1_lo):
                        x.passed(6)
                    lo2_done.passed(6 * KC)

        def wkv_phase():
            scr, zscr = t["scratch"], t["z_scratch"]
            NC = S // CHUNK
            W8 = [P, PAIRS, CHUNK]
            with ExitStack() as c:
                def st(name):
                    return sb(name, W8, c=c)

                def bd(name):
                    x = sb(name, [P, PAIRS, P], c=c)
                    diagonals.append(x)
                    return x

                diagonals = []
                rt, kt_, vt_, st_, at_ = st("r"), st("k"), st("v"), st("decay_sig"), st("a")
                vbd = bd("v_bd")
                kk, rn, k2, lcum, lprev = st("kk"), st("rn"), st("k2"), st("lcum"), st("lprev")
                ep, em, eq, bb, rk, sq = st("e_pos"), st("e_neg"), st("e_prev"), st("b"), st("rk"), st("kk_sq")
                ar = sb("ar", [P, PAIRS, 2, CHUNK], c=c)
                bbd, kbd, ntbd = bd("b_bd"), bd("k_bd"), bd("n_t")
                ntm = [sb(f"n_t_level{b}", [P, PAIRS, P], c=c) for b in range(2)]
                tst, rst, wst, wbd = st("inv"), st("inv_t"), st("one_plus"), bd("one_plus_bd")
                abd, rbd = [bd(f"a_bd{b}") for b in range(2)], [bd(f"r_bd{b}") for b in range(2)]
                aak, arb, ark = ([bd(f"{x}{b}") for b in range(2)] for x in ("a_k", "r_b", "r_k"))
                inv = [bd(f"inv_t_bd{b}") for b in range(2)]
                btok, ktok = [bd(f"b_tok{b}") for b in range(2)], [bd(f"k_tok{b}") for b in range(2)]
                vtok, gt, bonus = ([st(f"{x}{b}") for b in range(2)] for x in ("v_tok", "gate", "bonus"))
                pend = [sb(f"p_end{b}", [P, PAIRS], c=c) for b in range(2)]
                state, xst, ust = st("state"), st("x_st"), st("u_st")
                yc, ysq, ybd, z = st("y_centred"), st("y_sq"), bd("y_bd"), st("z")
                mean, var = sb("mean", [P, PAIRS], c=c), sb("var", [P, PAIRS], c=c)
                reset, reset_in = sb("reset", [P, HALF], c=c), sig("reset_in", 16)
                DEC = math.exp(-0.5)

                names = ("tiles_in g_in kk_done t1_done l_done mx_done rn_done ar_done bk_done bonus_done nt_done g_out "
                         "sq_done_w ss_done rt_done_w e_done eq_done bd_done tok_out ka_step k2_done lq_done kkn_done b_done "
                         "rk_step rk_done bonus_ps g1_done g2_done tok_done lev_mask x_done_w w_done tr_done t_done "
                         "xs_done xe_done us_done ue_done sn_done s_step s_done y_done_w m_step yc_done ysq_done var_done "
                         "yrt_done yrn_done ybd_done yf_done z1_done z_step zeros").split()
                g = {n: sig("wkv_" + n, 16 if n in ("tiles_in", "g_in") else 1) for n in names}
                chunk_used = [sig(f"chunk_used{b}") for b in range(2)]
                post_done = [sig(f"post_done{b}") for b in range(2)]
                z_stored = sig("z_stored", 16)
                idst = con[:, C_IDST:C_IDST + CHUNK]

                def flat(x):
                    return x.rearrange("p a n -> p (a n)")

                def per_pair(cols):
                    return cols.unsqueeze(2).to_broadcast(W8)

                def column(v):
                    return per_pair(vec[:, v:v + PAIRS])

                def bank(b, j0=0, j1=PAIRS):
                    return ps[:, b, j0 * CHUNK:j1 * CHUNK].rearrange("p (a n) -> p a n", n=CHUNK)

                def halves(x, pairs=slice(0, PAIRS)):
                    return [(slice(h * HEAD, (h + 1) * HEAD), x[h * HEAD:(h + 1) * HEAD, pairs, h * HEAD:(h + 1) * HEAD])
                            for h in range(2)]

                QP = PAIRS // 2
                NL = len(LEVELS)

                def schedule(eng, first, both, second):
                    first(0, 0, 0)
                    with eng.Fori(0, NC // 2 - 1) as i:
                        both((2 * i + 1, i, 1), (2 * i, i, 0))
                        both((2 * i + 2, i + 1, 0), (2 * i + 1, i, 1))
                    both((NC - 1, NC // 2 - 1, 1), (NC - 2, NC // 2 - 1, 0))
                    second(NC - 1, NC // 2 - 1, 1)

                with nc.Block() as block:
                    @block.sync
                    def _(sp):
                        sp.dma_start(reset[:, :], t["consts"][:, C_RESET:C_ALL]).then_inc(*reset_in.up)
                        sp.wait_ge(*g["zeros"].at(1))

                        def first(ch, i, b):
                            sp.wait_ge(*g["bonus_done"].at(ch))
                            sp.wait_ge(*g["tok_out"].at(3 * ch))
                            settle(sp)
                            for n, x in enumerate((rt, kt_, vt_, st_, at_)):
                                sp.dma_start(x[:, :, :], scr[n, bass.ds(ch, 1)].rearrange("c p a n -> (c p) a n")).then_inc(*g["tiles_in"].up)
                            for h in range(2):
                                hs = slice(h * HEAD, (h + 1) * HEAD)
                                sp.dma_start(vbd[hs, :, hs], scr[2, bass.ds(ch, 1), hs].rearrange("c p a n -> (c p) a n")).then_inc(*g["tiles_in"].up)
                            sp.wait_ge(*post_done[b].at(i))
                            settle(sp)
                            sp.dma_start(gt[b][:, :, :], scr[5, bass.ds(ch, 1)].rearrange("c p a n -> (c p) a n")).then_inc(*g["g_in"].up)

                        def second(ch, i, b):
                            sp.wait_ge(*post_done[b].at(i + 1))
                            settle(sp)
                            sp.dma_start(zscr[bass.ds(ch, 1)].rearrange("c p a n -> (c p) a n"), z[:, :, :]).then_inc(*z_stored.up)

                        schedule(sp, first, lambda x, y: (first(*x), second(*y)), second)
                        sp.wait_ge(*z_stored.at(NC))

                    @block.gpsimd
                    def _(pool):
                        for x in diagonals:
                            pool.memset(x[:, :, :], 0.0)
                        pool.memset(state[:, :, :], 0.0).then_inc(*g["zeros"].up)

                        def first(ch, i, b):
                            pool.wait_ge(*g["t1_done"].at(ch + 1))
                            pool.tensor_tensor(k2[:, :, :], k2[:, :, :], column(V_KA), ALU.mult).then_inc(*g["ka_step"].up)
                            pool.wait_ge(*g["ka_step"].at(ch + 1))
                            pool.tensor_tensor(k2[:, :, :], k2[:, :, :], kt_[:, :, :], ALU.add).then_inc(*g["k2_done"].up)
                            pool.wait_ge(*g["l_done"].at(ch + 1))
                            pool.tensor_tensor(lprev[:, :, :], lcum[:, :, :], st_[:, :, :], ALU.subtract).then_inc(*g["lq_done"].up)
                            pool.wait_ge(*g["rn_done"].at(ch + 1))
                            pool.tensor_tensor(kk[:, :, :], kk[:, :, :], rn[:, :, :], ALU.mult).then_inc(*g["kkn_done"].up)
                            pool.wait_ge(*g["kkn_done"].at(ch + 1))
                            pool.tensor_tensor(bb[:, :, :], kk[:, :, :], at_[:, :, :], ALU.mult).then_inc(*g["b_done"].up)
                            pool.wait_ge(*g["k2_done"].at(ch + 1))
                            pool.tensor_tensor(rk[:, :, :], rt[:, :, :], k2[:, :, :], ALU.mult).then_inc(*g["rk_step"].up)
                            pool.wait_ge(*g["rk_step"].at(ch + 1))
                            pool.tensor_tensor(rk[:, :, :], rk[:, :, :], column(V_RK), ALU.mult).then_inc(*g["rk_done"].up)

                        def level_mask(ch, l):
                            if l == 0:
                                pool.wait_ge(*g["nt_done"].at(ch + 1))
                            pool.wait_ge(*g["x_done_w"].at(2 * NL * ch + 2 * l - 2 if l >= 2 else 2 * NL * ch))
                            m = con[:, C_LEVEL + l * P:C_LEVEL + (l + 1) * P].unsqueeze(1).to_broadcast([P, PAIRS, P])
                            pool.tensor_tensor(ntm[l % 2][:, :, :], ntbd[:, :, :], m, ALU.mult).then_inc(*g["lev_mask"].up)

                        def levels(ch):
                            for l in range(NL):
                                level_mask(ch, l)

                        def second(ch, i, b):
                            pool.wait_ge(*g["z1_done"].at(ch + 1))
                            pool.tensor_tensor(z[:, :, :], z[:, :, :], column(V_LNB), ALU.add).then_inc(*g["z_step"].up)
                            pool.wait_ge(*g["z_step"].at(2 * ch + 1))
                            pool.tensor_tensor(z[:, :, :], z[:, :, :], bonus[b][:, :, :], ALU.add).then_inc(*g["z_step"].up)
                            pool.wait_ge(*g["z_step"].at(2 * ch + 2))
                            pool.wait_ge(*g["g_in"].at(ch + 1))
                            pool.tensor_tensor(z[:, :, :], z[:, :, :], gt[b][:, :, :], ALU.mult).then_inc(*post_done[b].up)

                        schedule(pool, lambda *x: (first(*x), levels(x[0])),
                                 lambda x, y: (first(*x), levels(x[0]), second(*y)), second)

                    @block.scalar
                    def _(act):
                        def first(ch, i, b):
                            act.wait_ge(*g["kk_done"].at(ch + 1))
                            act.activation(sq[:, :, :], kk[:, :, :], ACT.Square).then_inc(*g["sq_done_w"].up)
                            act.wait_ge(*g["mx_done"].at(ch + 1))
                            act.activation(rn[:, :, :], rn[:, :, :], ACT.Sqrt).then_inc(*g["rt_done_w"].up)
                            act.wait_ge(*g["l_done"].at(ch + 1))
                            act.activation(ep[:, :, :], lcum[:, :, :], ACT.Exp, scale=-DEC).then_inc(*g["e_done"].up)
                            act.activation(em[:, :, :], lcum[:, :, :], ACT.Exp, scale=DEC).then_inc(*g["e_done"].up)
                            act.wait_ge(*g["lq_done"].at(ch + 1))
                            act.activation(eq[:, :, :], lprev[:, :, :], ACT.Exp, scale=-DEC).then_inc(*g["eq_done"].up)
                            act.wait_ge(*g["e_done"].at(2 * ch + 2))
                            act.wait_ge(*post_done[b].at(i))
                            act.activation(pend[b][:, :].unsqueeze(2), ep[:, :, CHUNK - 1:CHUNK], ACT.Copy)
                            act.wait_ge(*g["ar_done"].at(2 * ch + 2))
                            act.wait_ge(*chunk_used[b].at(i))
                            for x, src in ((abd[b], 0), (rbd[b], 1)):
                                for hs, dst in halves(x):
                                    last = act.activation(dst, ar[hs, :, src, :], ACT.Copy)
                            last.then_inc(*g["bd_done"].up)

                        def tokens(ch, i, b):
                            for n, x in enumerate((btok[b], ktok[b])):
                                act.wait_ge(*g["tok_done"].at(3 * ch + n + 1))
                                for hs, dst in halves(x):
                                    last = act.activation(dst, ps[hs, 4 + n, :].rearrange("p (a n) -> p a n", n=CHUNK), ACT.Copy)
                                last.then_inc(*g["tok_out"].up)
                            act.wait_ge(*g["tok_done"].at(3 * ch + 3))
                            act.activation(vtok[b][:, :, :], bank(4), ACT.Copy).then_inc(*g["tok_out"].up)

                        def level(ch, b, l, q):
                            pairs = slice(q * QP, (q + 1) * QP)
                            act.wait_ge(*g["tr_done"].at(2 * NL * ch + 2 * l + q + 1))
                            if 0 < l < NL - 1:
                                act.activation(tst[:, pairs, :], bank(2 + q, 0, QP), ACT.Copy)
                            if l < NL - 1:
                                act.activation(rst[:, pairs, :], bank(2 + q, QP, PAIRS), ACT.Copy)
                            for hs, dst in halves(inv[b], pairs):
                                last = act.activation(dst, bank(2 + q, QP, PAIRS)[hs], ACT.Copy)
                            last.then_inc(*g["t_done"].up)

                        def square(ch):
                            act.wait_ge(*g["yc_done"].at(ch + 1))
                            act.activation(ysq[:, :, :], yc[:, :, :], ACT.Square).then_inc(*g["ysq_done"].up)

                        def root(ch):
                            act.wait_ge(*g["var_done"].at(ch + 1))
                            act.activation(var[:, :], var[:, :], ACT.Sqrt, scale=1.0 / HEAD,
                                                            bias=con[:, C_GNEPS:C_GNEPS + 1]).then_inc(*g["yrt_done"].up)

                        def alone(ch, i, b):
                            first(ch, i, b), tokens(ch, i, b)
                            for l in range(NL):
                                level(ch, b, l, 0), level(ch, b, l, 1)

                        def both(x, y):
                            first(*x), tokens(*x)
                            for l in range(NL):
                                level(x[0], x[2], l, 0), level(x[0], x[2], l, 1)
                                if l == 2:
                                    square(y[0])
                                if l == 3:
                                    root(y[0])

                        act.wait_ge(*g["zeros"].at(1))
                        schedule(act, alone, both, lambda ch, i, b: (square(ch), root(ch)))

                    @block.tensor
                    def _(pe):
                        def first(ch, i, b):
                            pe.wait_ge(*g["sq_done_w"].at(ch + 1))
                            pe.wait_ge(*g["tok_out"].at(3 * ch))
                            pe.matmul(ps[:, 4, :], con[:, C_BLOCK:C_BLOCK + P], flat(sq[:, :, :]), start=True, stop=True).then_inc(*g["ss_done"].up)
                            pe.wait_ge(*g["rk_done"].at(ch + 1))
                            pe.matmul(ps[:, 5, :], con[:, C_BLOCK:C_BLOCK + P], flat(rk[:, :, :]), start=True, stop=True).then_inc(*g["bonus_ps"].up)
                            pe.wait_ge(*g["t_done"].at(2 * NL * ch))
                            pe.wait_ge(*g["bd_done"].at(ch + 1))
                            pe.wait_ge(*g["bk_done"].at(ch + 1))
                            for n, x in enumerate((bbd, kbd)):
                                for j in range(PAIRS):
                                    ins = pe.matmul(ps[:, 2 * n + j // 4, (j % 4) * P:(j % 4 + 1) * P], x[:, j, :],
                                                    ar[:, j, :, :].rearrange("p a n -> p (a n)"), start=True, stop=True)
                                ins.then_inc(*g[f"g{n + 1}_done"].up)
                            pe.wait_ge(*g["bonus_done"].at(ch + 1))
                            for n, (x, bk) in enumerate(((bbd, 4), (kbd, 5), (vbd, 4))):
                                if n == 2:
                                    pe.wait_ge(*g["tok_out"].at(3 * ch + 1))
                                for j in range(PAIRS):
                                    ins = pe.matmul(bank(bk)[:, j, :], x[:, j, :], idst, start=True, stop=True)
                                ins.then_inc(*g["tok_done"].up)

                        def level(ch, b, l):
                            base = 2 * NL * ch + 2 * l
                            pe.wait_ge(*g["lev_mask"].at(NL * ch + l + 1))
                            if l == 0:
                                pe.wait_ge(*g["g_out"].at(ch + 1))
                            for q in range(2):
                                if l > 0:
                                    pe.wait_ge(*g["t_done"].at(base - 1 + q))
                                for j in range(QP):
                                    jj = q * QP + j
                                    ins = pe.matmul(bank(q)[:, j, :], ntm[l % 2][:, jj, :], tst[:, jj, :] if l else idst,
                                                    start=True, stop=True)
                                ins.then_inc(*g["x_done_w"].up)
                            for q in range(2):
                                pe.wait_ge(*g["w_done"].at(base + q + 1))
                                for j in range(QP):
                                    jj = q * QP + j
                                    if 0 < l < NL - 1:
                                        pe.matmul(bank(2 + q)[:, j, :], inv[b][:, jj, :], wst[:, jj, :], start=True, stop=True)
                                for j in range(QP):
                                    jj = q * QP + j
                                    ins = pe.matmul(bank(2 + q)[:, QP + j, :], wbd[:, jj, :], rst[:, jj, :] if l else idst,
                                                    start=True, stop=True)
                                ins.then_inc(*g["tr_done"].up)

                        def solve_x(ch, i, b):
                            pe.wait_ge(*g["s_done"].at(ch))
                            pe.wait_ge(*g["g_out"].at(ch + 1))
                            pe.wait_ge(*g["tok_out"].at(3 * ch + 3))
                            for j in range(PAIRS):
                                pe.matmul(bank(6)[:, j, :], aak[b][:, j, :], vtok[b][:, j, :], start=True, stop=False)
                                ins = pe.matmul(bank(6)[:, j, :], abd[b][:, j, :], state[:, j, :], start=False, stop=True)
                            ins.then_inc(*g["xs_done"].up)

                        def solve_u(ch, i, b):
                            pe.wait_ge(*g["t_done"].at(2 * NL * (ch + 1)))
                            pe.wait_ge(*g["xe_done"].at(ch + 1))
                            for j in range(PAIRS):
                                ins = pe.matmul(bank(6)[:, j, :], inv[b][:, j, :], xst[:, j, :], start=True, stop=True)
                            ins.then_inc(*g["us_done"].up)

                        def outputs(ch, i, b):
                            pe.wait_ge(*g["ue_done"].at(ch + 1))
                            pe.wait_ge(*g["z1_done"].at(ch))
                            for j in range(PAIRS):
                                pe.matmul(bank(7)[:, j, :], rbd[b][:, j, :], state[:, j, :], start=True, stop=False)
                                pe.matmul(bank(7)[:, j, :], ark[b][:, j, :], vtok[b][:, j, :], start=False, stop=False)
                                ins = pe.matmul(bank(7)[:, j, :], arb[b][:, j, :], ust[:, j, :], start=False, stop=True)
                            ins.then_inc(*g["y_done_w"].up)
                            for j in range(PAIRS):
                                pe.matmul(bank(6)[:, j, :], ktok[b][:, j, :], vtok[b][:, j, :], start=True, stop=False)
                                ins = pe.matmul(bank(6)[:, j, :], btok[b][:, j, :], ust[:, j, :], start=False, stop=True)
                            ins.then_inc(*chunk_used[b].up)

                        def by_feature(ch):
                            pe.wait_ge(*g["ybd_done"].at(ch + 1))
                            for j in range(PAIRS):
                                ins = pe.matmul(bank(7)[:, j, :], ybd[:, j, :], idst, start=True, stop=True)
                            ins.then_inc(*g["yf_done"].up)

                        def alone(ch, i, b):
                            first(ch, i, b)
                            for l in range(NL):
                                level(ch, b, l)

                        def both(x, y):
                            first(*x)
                            for l in range(NL):
                                level(x[0], x[2], l)
                                if l == 0:
                                    solve_x(*y)
                                if l == 1:
                                    solve_u(*y)
                                if l == 2:
                                    outputs(*y)
                                if l == 5:
                                    by_feature(y[0])

                        pe.wait_ge(*g["zeros"].at(1))
                        schedule(pe, alone, both, lambda *y: (solve_x(*y), solve_u(*y), outputs(*y), by_feature(y[0])))

                    @block.vector
                    def _(dve):
                        def first(ch, i, b):
                            dve.wait_ge(*g["tiles_in"].at(7 * ch + 7))
                            dve.tensor_tensor(kk[:, :, :], kt_[:, :, :], column(V_KK), ALU.mult).then_inc(*g["kk_done"].up)
                            dve.scalar_tensor_tensor(k2[:, :, :], at_[:, :, :], 1.0, kt_[:, :, :], ALU.subtract, ALU.mult).then_inc(*g["t1_done"].up)
                            dve.tensor_tensor_scan(flat(lcum[:, :, :]), reset[:, :],
                                                                  flat(st_[:, :, :]), 0.0, ALU.mult, ALU.add).then_inc(*g["l_done"].up)
                            dve.wait_ge(*g["ss_done"].at(ch + 1))
                            dve.tensor_scalar(rn[:, :, :], bank(4), 1e-24, None, ALU.max).then_inc(*g["mx_done"].up)
                            dve.wait_ge(*g["rt_done_w"].at(ch + 1))
                            dve.reciprocal(rn[:, :, :], rn[:, :, :]).then_inc(*g["rn_done"].up)
                            dve.wait_ge(*g["e_done"].at(2 * ch + 2))
                            dve.tensor_tensor(ar[:, :, 1, :], rt[:, :, :], ep[:, :, :], ALU.mult).then_inc(*g["ar_done"].up)
                            dve.wait_ge(*g["k2_done"].at(ch + 1))
                            for hs, dst in halves(kbd):
                                dve.tensor_tensor(dst, k2[hs, :, :], em[hs, :, :], ALU.mult)
                            dve.wait_ge(*g["eq_done"].at(ch + 1))
                            dve.wait_ge(*g["kkn_done"].at(ch + 1))
                            dve.scalar_tensor_tensor(ar[:, :, 0, :], kk[:, :, :], -1.0, eq[:, :, :], ALU.mult, ALU.mult).then_inc(*g["ar_done"].up)
                            dve.wait_ge(*g["b_done"].at(ch + 1))
                            for hs, dst in halves(bbd):
                                last = dve.tensor_tensor(dst, bb[hs, :, :], em[hs, :, :], ALU.mult)
                            last.then_inc(*g["bk_done"].up)
                            dve.wait_ge(*g["bonus_ps"].at(ch + 1))
                            dve.wait_ge(*post_done[b].at(i))
                            dve.tensor_tensor(bonus[b][:, :, :], bank(5), vt_[:, :, :], ALU.mult).then_inc(*g["bonus_done"].up)

                            def masked(out, n, which, mask):
                                for hs, dst in halves(out):
                                    for j in range(2):
                                        src = ps[hs, 2 * n + j, :].rearrange("p (a s n) -> p a s n", s=2, n=CHUNK)[:, :, which, :]
                                        m = con[hs, mask:mask + CHUNK].unsqueeze(1).to_broadcast([HEAD, 4, CHUNK])
                                        last = dve.tensor_tensor(dst[:, 4 * j:4 * j + 4, :], src, m, ALU.mult)
                                return last

                            dve.wait_ge(*g["g1_done"].at(ch + 1))
                            dve.wait_ge(*g["lev_mask"].at(NL * ch))
                            masked(ntbd, 0, 0, C_STRICT).then_inc(*g["nt_done"].up)
                            dve.wait_ge(*chunk_used[b].at(i))
                            masked(arb[b], 0, 1, C_CAUSAL)
                            dve.wait_ge(*g["g2_done"].at(ch + 1))
                            masked(aak[b], 1, 0, C_STRICT)
                            masked(ark[b], 1, 1, C_CAUSAL).then_inc(*g["g_out"].up)

                        def level(ch, l, q):
                            pairs = slice(q * QP, (q + 1) * QP)
                            dve.wait_ge(*g["x_done_w"].at(2 * NL * ch + 2 * l + q + 1))
                            one = idst.unsqueeze(1).to_broadcast([P, QP, CHUNK])
                            if l < NL - 1:
                                out = wst if l else tst
                                dve.tensor_tensor(out[:, pairs, :], bank(q, 0, QP), one, ALU.add)
                            for hs, dst in halves(wbd, pairs):
                                last = dve.tensor_tensor(dst, bank(q, 0, QP)[hs], one[hs], ALU.add)
                            last.then_inc(*g["w_done"].up)

                        def take_x(ch):
                            dve.wait_ge(*g["xs_done"].at(ch + 1))
                            dve.tensor_copy(xst[:, :, :], bank(6)).then_inc(*g["xe_done"].up)

                        def take_u(ch):
                            dve.wait_ge(*g["us_done"].at(ch + 1))
                            dve.tensor_copy(ust[:, :, :], bank(6)).then_inc(*g["ue_done"].up)

                        def new_state(ch, i, b):
                            dve.wait_ge(*chunk_used[b].at(i + 1))
                            dve.tensor_tensor(state[:, :, :], bank(6), state[:, :, :], ALU.add).then_inc(*g["s_step"].up)
                            dve.wait_ge(*g["s_step"].at(ch + 1))
                            dve.tensor_tensor(state[:, :, :], state[:, :, :], per_pair(pend[b][:, :]), ALU.mult).then_inc(*g["s_done"].up)

                        def centre(ch):
                            dve.wait_ge(*g["y_done_w"].at(ch + 1))
                            dve.tensor_reduce(mean[:, :], bank(7), AX.X, ALU.add).then_inc(*g["m_step"].up)
                            dve.wait_ge(*g["m_step"].at(2 * ch + 1))
                            dve.tensor_scalar(mean[:, :], mean[:, :], -1.0 / HEAD, None, ALU.mult).then_inc(*g["m_step"].up)
                            dve.wait_ge(*g["m_step"].at(2 * ch + 2))
                            dve.tensor_tensor(yc[:, :, :], bank(7), per_pair(mean[:, :]), ALU.add).then_inc(*g["yc_done"].up)

                        def variance(ch):
                            dve.wait_ge(*g["ysq_done"].at(ch + 1))
                            dve.tensor_reduce(var[:, :], ysq[:, :, :], AX.X, ALU.add).then_inc(*g["var_done"].up)

                        def scale(ch):
                            dve.wait_ge(*g["yrt_done"].at(ch + 1))
                            dve.reciprocal(var[:, :], var[:, :]).then_inc(*g["yrn_done"].up)
                            dve.wait_ge(*g["yrn_done"].at(ch + 1))
                            for hs, dst in halves(ybd):
                                last = dve.tensor_tensor(dst, yc[hs, :, :], per_pair(var[:, :])[hs], ALU.mult)
                            last.then_inc(*g["ybd_done"].up)

                        def affine(ch):
                            dve.wait_ge(*g["yf_done"].at(ch + 1))
                            dve.wait_ge(*z_stored.at(ch))
                            dve.tensor_tensor(z[:, :, :], bank(7), column(V_LNW), ALU.mult).then_inc(*g["z1_done"].up)

                        def alone(ch, i, b):
                            first(ch, i, b)
                            for l in range(NL):
                                level(ch, l, 0), level(ch, l, 1)

                        def both(x, y):
                            first(*x)
                            for l in range(NL):
                                level(x[0], l, 0), level(x[0], l, 1)
                                if l == 0:
                                    take_x(y[0])
                                if l == 1:
                                    take_u(y[0])
                                if l == 2:
                                    new_state(*y), centre(y[0])
                                if l == 3:
                                    variance(y[0])
                                if l == 4:
                                    scale(y[0])
                            affine(y[0])

                        dve.wait_ge(*g["zeros"].at(1))
                        dve.wait_ge(*reset_in.at(1))
                        schedule(dve, alone, both, lambda ch, i, b: (take_x(ch), take_u(ch), new_state(ch, i, b), centre(ch),
                                                                     variance(ch), scale(ch), affine(ch)))

        def split_phase(hi, lo):
            with ExitStack() as c:
                raw = [sb(f"z_raw{b}", [P, S], c=c) for b in range(2)]
                z_in = [sig(f"z_in{b}", 16) for b in range(2)]
                z_hi, z_lo = sig("z_hi"), sig("z_lo")
                with nc.Block() as block:
                    @block.sync
                    def _(sp):
                        for k in range(KC):
                            if k >= 2:
                                sp.wait_ge(*z_lo.at(k - 1))
                            sp.dma_start(raw[k % 2][:, :].rearrange("p (c n) -> p c n", n=CHUNK),
                                                        t["z_scratch"][:, :, k, :].rearrange("c p n -> p c n")).then_inc(*z_in[k % 2].up)

                    @block.scalar
                    def _(act):
                        for k in range(KC):
                            act.wait_ge(*z_in[k % 2].at(k // 2 + 1))
                            act.activation(hi[:, k, :], raw[k % 2][:, :], ACT.Copy).then_inc(*z_hi.up)

                    @block.vector
                    def _(dve):
                        for k in range(KC):
                            dve.wait_ge(*z_hi.at(k + 1))
                            dve.tensor_tensor(lo[:, k, :], raw[k % 2][:, :], hi[:, k, :].bitcast(F32), ALU.subtract).then_inc(*z_lo.up)
                z_in[0].passed(4), z_in[1].passed(4), z_hi.passed(KC), z_lo.passed(KC)

        def layer1():
            rwkv_projections()
            wkv_phase()
            with ExitStack() as c:
                hi, lo = sb("hi", [P, KC, S], F32R, c), sb("lo", [P, KC, S], F32R, c)
                split_phase(hi, lo)
                with ExitStack() as c2:
                    w = Weights(sb, c2)
                    out_phase(w, t["rk_w_out"], (6 + 2) * KC, hi, lo)
                norm_phase(3, hi, lo)
                ffn_phase(1, hi, lo)

        ada_phase()
        def layer0():
            with ExitStack() as c:
                hi, lo = sb("hi", [P, KC, S], F32R, c), sb("lo", [P, KC, S], F32R, c)
                norm_phase(0, hi, lo)
                with ExitStack() as c2:
                    w = Weights(sb, c2)
                    qk, vt = sb("qk", [P, QCH + KCH, S], c=c2), sb("vt", [P, NT, VDIM], c=c2)
                    with ExitStack() as c3:
                        cos, sin = sb("cos", [P, S], c=c3), sb("sin", [P, S], c=c3)
                        rope_phase(cos, sin)
                        qkv_phase(w, hi, lo, cos, sin, qk, vt)
                    attention_phase(qk, vt, hi, lo)
                    out_phase(w, t["attn_w_out"], 2 * KC, hi, lo)
                norm_phase(1, hi, lo)
                ffn_phase(0, hi, lo)

        layer0()
        layer1()
        with nc.Block() as block:
            stored = sig("stored", 16)

            @block.sync
            def _(sp):
                sp.dma_start(t["outT"], xt[:, :, :]).then_inc(*stored.up)
                sp.wait_ge(*stored.at(1))


def constants():
    con = np.zeros((P, C_ALL), np.float32)
    r = np.arange(P)
    con[:, C_IDENT:C_IDENT + P] = np.eye(P)
    con[:, C_ONES:C_ONES + P] = 1.0
    con[:, C_BLOCK:C_BLOCK + P] = r[:, None] // HEAD == r[None, :] // HEAD
    for m in r:
        if m % HEAD < HEAD // 2:
            con[m + HEAD // 2, C_ROT + m] = -1.0
        else:
            con[m - HEAD // 2, C_ROT + m] = 1.0
    i, j = (r % CHUNK)[:, None], np.arange(CHUNK)[None, :]
    con[:, C_IDST:C_IDST + CHUNK] = i == j
    con[:, C_STRICT:C_STRICT + CHUNK] = j > i
    con[:, C_CAUSAL:C_CAUSAL + CHUNK] = j >= i
    con[:, C_RESET:C_RESET + HALF] = np.arange(HALF) % CHUNK != 0
    chunk = np.arange(BAND)[None, :] // CHUNK - (r // CHUNK)[:, None]
    con[:, C_BAND:C_BAND + BAND] = np.where((chunk >= 0) & (chunk <= 1), 0.0, NEG)
    for n, size in enumerate(LEVELS):
        src, dst = r[:, None], r[None, :]
        con[:, C_LEVEL + n * P:C_LEVEL + (n + 1) * P] = ((src // (2 * size) == dst // (2 * size))
                                                        & (src // size % 2 == 0) & (dst // size % 2 == 1))
    freq = np.float32(10000.0) ** (-np.arange(0, HEAD, 2, dtype=np.float32) / np.float32(HEAD))
    con[:, C_FREQ] = freq[r % (HEAD // 2)]
    con[:, C_EPS] = EPS
    con[:, C_GNEPS] = GN_EPS
    return con


def layout(x, c, positions, ada_w, ada_b, norm1_g, norm2_g,
           attn_w_in, attn_w_out, attn_q_norm, attn_k_norm, attn_sinks,
           rk_mu, rk_w_rkv, rk_w0, rk_w1, rk_w2, rk_a0, rk_a1, rk_a2,
           rk_v0, rk_v1, rk_v2, rk_g1, rk_g2, rk_k_k, rk_k_a, rk_r_k,
           rk_ln_w, rk_ln_b, rk_w_out, ffn_w_in, ffn_w_out):
    def cols(v):
        return np.asarray(v).reshape(-1, P).T

    def tiles(m):
        k, n = m.shape
        return np.ascontiguousarray(m.reshape(k // P, P, n // P, P).transpose(2, 1, 0, 3))

    order = [GROUP * (2 * (j // GROUP) + s) + j % GROUP for j in range(QCH) for s in range(2)]
    sinks = np.asarray(attn_sinks[0])
    w_in = np.asarray(attn_w_in[0])
    wq = w_in[:, :D].reshape(D, 16, HEAD)[:, order].reshape(D, D)
    wk, wv = w_in[:, D:D + VDIM], w_in[:, D + VDIM:]
    w_out = np.asarray(attn_w_out[0]).reshape(16, HEAD, D)[order].reshape(D, D)
    vecs = np.concatenate(
        [cols(ada_b), np.concatenate([cols(g[l]) for l in range(DEPTH) for g in (norm1_g, norm2_g)], 1),
         cols(rk_mu[0]), cols(rk_w0[0]), cols(rk_a0[0]), cols(rk_k_k[0]), cols(rk_k_a[0]), cols(rk_r_k[0]),
         cols(rk_ln_w[0]), cols(rk_ln_b[0])]
        + [cols(np.tile(attn_q_norm[0], 2))] * QCH + [cols(np.tile(attn_k_norm[0], 2))] * KCH
        + [cols(c[0]), np.broadcast_to(sinks, (P, 16))], 1)

    def padded(m, rows, columns):
        out = np.zeros((rows, columns), m.dtype)
        out[:m.shape[0], :m.shape[1]] = m
        return out

    lora1 = [padded(np.asarray(m[0]), D, P) for m in (rk_w1, rk_a1, rk_g1)]
    lora2 = [padded(np.asarray(m[0]), P, D) for m in (rk_w2, rk_a2, rk_g2)]
    ffn_in = np.asarray(ffn_w_in).reshape(DEPTH, KC, P, 2, FITER * FS, P).transpose(0, 4, 2, 1, 3, 5)
    ffn_out = np.asarray(ffn_w_out).reshape(DEPTH, FITER, FS, P, D).transpose(0, 1, 3, 2, 4)
    arrays = {
        "xT": np.asarray(x[0]).T.reshape(KC, P, S).transpose(1, 0, 2),
        "positions": np.broadcast_to(np.asarray(positions), (P, S)),
        "vecs": vecs,
        "consts": constants(),
        "ada_w": np.asarray(ada_w).reshape(DEPTH, KC, P, 6, D).transpose(0, 3, 2, 1, 4).reshape(DEPTH * 6, P, KC, D),
        "wqk": tiles(np.concatenate([wq, wk], 1)),
        "wv": tiles(wv),
        "attn_w_out": tiles(w_out),
        "w_rkv": np.concatenate([tiles(np.asarray(rk_w_rkv[0][p])) for p in range(3)]),
        "lora1": np.concatenate([tiles(m) for m in lora1]),
        "lora2": np.stack([m.reshape(P, KC, P) for m in lora2]),
        "rk_w_out": tiles(np.asarray(rk_w_out[0])),
        "ffn_w_in": ffn_in.reshape(DEPTH * FITER * FS, P, KC, 2 * P),
        "ffn_w_out": ffn_out.reshape(DEPTH * FITER, P, FS, D),
    }
    return {k: np.ascontiguousarray(v) for k, v in arrays.items()}


def kernel(**inputs):
    import concourse.bacc as bacc
    from concourse.bass_utils import run_bass_kernel_spmd

    arrays = layout(**{k: np.asarray(v) for k, v in inputs.items()})
    nc = bacc.Bacc("TRN2", target_bir_lowering=False, num_devices=1)
    t = {k: nc.dram_tensor(f"in_{k}", a.shape, mybir.dt.from_np(a.dtype), kind="ExternalInput").ap()
         for k, a in arrays.items()}
    t["outT"] = nc.dram_tensor("outT", (P, KC, S), F32, kind="ExternalOutput").ap()
    t["scratch"] = nc.dram_tensor("scratch", (6, S // CHUNK, P, KC, CHUNK), F32, kind="Internal").ap()
    t["z_scratch"] = nc.dram_tensor("z_scratch", (S // CHUNK, P, KC, CHUNK), F32, kind="Internal").ap()
    build_program(nc, t)
    r = run_bass_kernel_spmd(nc, [{f"in_{k}": a for k, a in arrays.items()}], core_ids=[0])
    out = r.results[0]["outT"]
    return np.ascontiguousarray(out.transpose(1, 0, 2).reshape(D, S).T)[None]
```

```python
import math
from contextlib import ExitStack

import numpy as np
import concourse.bass as bass
from concourse import mybir

F32 = mybir.dt.float32
F32R = mybir.dt.float32r
I32 = mybir.dt.int32
ALU = mybir.AluOpType
ACT = mybir.ActivationFunctionType
AX = mybir.AxisListType

P = 128
D = 1024
S = 1024
KC = D // P
HALF = 512
NH = S // HALF
DEPTH = 2
HEAD = 64
QCH = 8
KCH = 2
GROUP = 4
VDIM = 256
CHUNK = 64
BAND = 3 * CHUNK
NT = S // P
FH = 2816
FSTEP = 256
FITER = FH // FSTEP
FS = FSTEP // P
PAIRS = KC
LEVELS = [1, 2, 4, 8, 16, 32]
EPS = 1e-6
GN_EPS = 64e-5
NEG = -1e30
TWO_PI = 2.0 * math.pi
PI_A = 6.28125
PI_B = float(np.float32(0.0019350051879882812))
PI_C = float(np.float32(TWO_PI - PI_A - PI_B))
ROUND = 12582912.0
ANG_MAX = 3.1415925

V_ADAB = 0
V_GAIN = V_ADAB + DEPTH * 6 * KC
V_MU = V_GAIN + 2 * DEPTH * KC
V_W0 = V_MU + 6 * KC
V_A0 = V_W0 + KC
V_KK = V_A0 + KC
V_KA = V_KK + KC
V_RK = V_KA + KC
V_LNW = V_RK + KC
V_LNB = V_LNW + KC
V_QKG = V_LNB + KC
V_C = V_QKG + QCH + KCH
V_SINK = V_C + KC
V_END = V_SINK + 16

C_IDENT = 0
C_ONES = C_IDENT + P
C_BLOCK = C_ONES + P
C_ROT = C_BLOCK + P
C_IDST = C_ROT + P
C_STRICT = C_IDST + CHUNK
C_CAUSAL = C_STRICT + CHUNK
C_BAND = C_CAUSAL + CHUNK
C_LEVEL = C_BAND + BAND
C_FREQ = C_LEVEL + len(LEVELS) * P
C_EPS = C_FREQ + 1
C_GNEPS = C_EPS + 1
C_END = C_GNEPS + 1
C_RESET = C_END
C_ALL = C_RESET + HALF


SIGNALS = """
tables*16 w_loaded0*16 w_loaded1*16 w_hi_done0 w_hi_done1 w_lo_done0 w_lo_done1 w_used0 w_used1
xin*16 slab_in0*16 slab_in1*16 slab_used0 slab_used1 cact_done mod_done mod_vec acc_step summed
sq_done ms_step ms_done rt_done rs_done xn_done h_done h_hi h_lo pos_in*16 ang_step/wkv_kk_done
red_done/wkv_t1_done trig_done/wkv_l_done qk_main/wkv_mx_done qk_sq/wkv_rn_done qk_aux/wkv_ar_done
qk_rt/wkv_bb_done qk_step/wkv_kb_done qk_out/wkv_bonus_done v_done/wkv_nt_done v_out/wkv_arb_done
q_staged/wkv_g_out v_staged/wkv_sq_done_w pb_zeroed/wkv_ss_done sc_done/wkv_rt_done_w
tp_done/wkv_e_done pv_done/wkv_eq_done a_step/wkv_pend_done nm_done/wkv_bd_done exp_done/wkv_v_tok
b_step/wkv_b_tok p_done/wkv_k_tok cur_out/wkv_v_out prev_out/wkv_b_out o_hi/wkv_k_out
o_lo/wkv_ka_step y_done x_done w1_in0*16 w1_in1*16 w1_hi_done0 w1_hi_done1 w1_lo_done0 w1_lo_done1
w2_in*16 w2_hi_done w2_lo_done w2_used up_done silu_done act_step act_done ffn_y ffn_x xx_done mix_f
mix_hi mix_lo taken0 taken1 stored0*16 stored1*16 lora1_done lora1_act lora1_step lora1_lo
lora2_done reset_in*16 wkv_tiles_in*16 wkv_v_in*16 wkv_k2_done wkv_lq_done wkv_kkn_done wkv_b_done
wkv_rk_step wkv_rk_done wkv_bonus_ps wkv_g1_done wkv_g2_done wkv_lev_mask wkv_inv_one wkv_x_done_w
wkv_w_done wkv_tr_done wkv_t_done wkv_xs_done wkv_xe_done wkv_us_done wkv_ue_done wkv_s_step
wkv_s_done wkv_y_done_w wkv_m_step wkv_yc_done wkv_ysq_done wkv_var_done wkv_yrt_done wkv_yrn_done
wkv_ybd_done wkv_yf_done wkv_z1_done wkv_bias_done wkv_z_step wkv_zeros g_in0*16 g_in1*16
chunk_used0 chunk_used1 post_done0 post_done1 z_stored*16 z_in0*16 z_in1*16 z_hi z_lo stored*16
"""


class Sig:

    def __init__(self, sem, unit=1):
        self.sem, self.unit, self.base = sem, unit, 1

    @property
    def up(self):
        return self.sem, self.unit

    def at(self, n):
        return self.sem, (self.base + n) * self.unit

    def passed(self, n):
        self.base += n


class Weights:

    def __init__(self, sb, c):
        self.raw = [sb(f"w_raw{s}", [P, KC, P], F32, c) for s in range(2)]
        self.hi = [sb(f"w_hi{s}", [P, KC, P], F32R, c) for s in range(2)]
        self.lo = [sb(f"w_lo{s}", [P, KC, P], F32R, c) for s in range(2)]


def build_program(nc, t):
    ctx = ExitStack()
    with ctx:
        stage = [0]

        def sb(name, shape, dt=F32, c=ctx):
            stage[0] += 1
            return c.enter_context(nc.sbuf_tensor(f"{name}_{stage[0]}", shape, dt))

        sems = {}

        def sig(name, unit=1):
            assert sems[name].unit == unit, name
            return sems[name]

        def settle(eng):
            eng.wait_ge(*tables.at(2))

        made = []
        for line in SIGNALS.split():
            names, _, unit = line.partition("*")
            made.append(Sig(ctx.enter_context(nc.semaphore(names.replace("/", "_or_"))), int(unit or 1)))
            for name in names.split("/"):
                sems[name] = made[-1]

        with nc.Block() as block:
            def signal_ahead(part):
                def program(eng):
                    for x in made[part::4]:
                        eng.sem_inc(x.sem, x.unit)
                return program

            block.sync(signal_ahead(0))
            block.vector(signal_ahead(1))
            block.scalar(signal_ahead(2))
            block.tensor(signal_ahead(3))

        ps = ctx.enter_context(nc.psum_tensor("ps", [P, 8, HALF], F32))
        xt = sb("xt", [P, KC, S])
        vec = sb("vec", [P, V_END])
        con = sb("con", [P, C_END])
        mod = sb("mod", [P, DEPTH * 6 * KC])
        gain = sb("gain", [P, 2 * DEPTH * KC])

        tables = sig("tables", 16)

        w_loaded = [sig(f"w_loaded{s}", 16) for s in range(2)]
        w_hi_done = [sig(f"w_hi_done{s}") for s in range(2)]
        w_lo_done = [sig(f"w_lo_done{s}") for s in range(2)]
        w_used = [sig(f"w_used{s}") for s in range(2)]
        slot_signals = [w_loaded, w_hi_done, w_lo_done, w_used]

        def load_weights(sp, w, s, i, src):
            sp.wait_ge(*w_lo_done[s].at(i))
            settle(sp)
            sp.dma_start(w.raw[s][:, :, :], src).then_inc(*w_loaded[s].up)

        def split_hi(act, w, s, i):
            act.wait_ge(*w_loaded[s].at(i + 1))
            act.wait_ge(*w_used[s].at(i))
            act.activation(w.hi[s][:, :, :], w.raw[s][:, :, :], ACT.Copy).then_inc(*w_hi_done[s].up)

        def split_lo(pool, w, s, i):
            pool.wait_ge(*w_hi_done[s].at(i + 1))
            pool.tensor_tensor(w.lo[s][:, :, :], w.raw[s][:, :, :],
                                               w.hi[s][:, :, :].bitcast(F32), ALU.subtract).then_inc(*w_lo_done[s].up)

        def product(pe, out, w_hi, w_lo, x_hi, x_lo, kc=KC, first=True, last=True):
            for k in range(kc):
                pe.matmul(out, w_hi(k), x_hi(k), start=first and k == 0, stop=False)
                pe.matmul(out, w_hi(k), x_lo(k), start=False, stop=False)
                ins = pe.matmul(out, w_lo(k), x_hi(k), start=False, stop=last and k == kc - 1)
            return ins

        def slots_passed(n):
            for group in slot_signals:
                for s in range(2):
                    group[s].passed(n)

        def ada_phase():
            with ExitStack() as c:
                slab = [sb(f"slab{s}", [P, KC, D], c=c) for s in range(2)]
                cact = sb("cact", [P, KC], c=c)
                acc = [sb(f"ada_acc{s}", [P, D], c=c) for s in range(2)]
                xin = sig("xin", 16)
                slab_in = [sig(f"slab_in{s}", 16) for s in range(2)]
                slab_used = [sig(f"slab_used{s}") for s in range(2)]
                cact_done, mod_done, mod_vec = sig("cact_done"), sig("mod_done"), sig("mod_vec")
                acc_step, summed = sig("acc_step"), sig("summed")
                with nc.Block() as block:
                    @block.sync
                    def _(sp):
                        sp.dma_start(vec[:, :], t["vecs"]).then_inc(*tables.up)
                        sp.dma_start(con[:, :], t["consts"][:, 0:C_END]).then_inc(*tables.up)
                        with sp.Fori(0, DEPTH * 3) as i:
                            for s in range(2):
                                sp.wait_ge(*slab_used[s].at(i))
                                settle(sp)
                                sp.dma_start(slab[s][:, :, :], t["ada_w"][bass.ds(2 * i + s, 1)].rearrange("a p k n -> (a p) k n")).then_inc(*slab_in[s].up)
                        sp.dma_start(xt[:, :, :], t["xT"]).then_inc(*xin.up)
                        sp.wait_ge(*xin.at(1))

                    @block.scalar
                    def _(act):
                        act.wait_ge(*tables.at(2))
                        act.activation(cact[:, :], vec[:, V_C:V_C + KC], ACT.Silu).then_inc(*cact_done.up)

                    @block.tensor
                    def _(pe):
                        with pe.Fori(0, DEPTH * 3) as i:
                            pe.wait_ge(*mod_done.at(2 * i))
                            for s in range(2):
                                pe.wait_ge(*slab_used[s].at(i + 1))
                                for j in range(KC):
                                    ins = pe.matmul(ps[:, s, j:j + 1], acc[s][:, j * P:(j + 1) * P],
                                                    con[:, C_ONES:C_ONES + 1], start=True, stop=True)
                                ins.then_inc(*summed.up)

                    @block.vector
                    def _(dve):
                        dve.wait_ge(*cact_done.at(1))
                        with dve.Fori(0, DEPTH * 3) as i:
                            for s in range(2):
                                dve.wait_ge(*slab_in[s].at(i + 1))
                                dve.tensor_scalar(acc[s][:, :], slab[s][:, 0, :], cact[:, 0:1], None, ALU.mult).then_inc(*acc_step.up)
                                for k in range(1, KC):
                                    dve.wait_ge(*acc_step.at(2 * (KC - 1) * i + (KC - 1) * s + k))
                                    ins = dve.scalar_tensor_tensor(acc[s][:, :], slab[s][:, k, :], cact[:, k:k + 1], acc[s][:, :],
                                                                   ALU.mult, ALU.add)
                                    ins.then_inc(*(acc_step if k < KC - 1 else slab_used[s]).up)
                            for s in range(2):
                                dve.wait_ge(*summed.at(2 * i + s + 1))
                                dve.tensor_tensor(mod[:, bass.ds((2 * i + s) * KC, KC)], ps[:, s, 0:KC],
                                                  vec[:, bass.ds(V_ADAB + (2 * i + s) * KC, KC)], ALU.add).then_inc(*mod_done.up)
                        dve.wait_ge(*mod_done.at(DEPTH * 6))
                        for n in range(2 * DEPTH):
                            sc = (n // 2) * 6 * KC + (3 * (n % 2) + 1) * KC
                            dve.scalar_tensor_tensor(
                                gain[:, n * KC:(n + 1) * KC], mod[:, sc:sc + KC], 1.0,
                                vec[:, V_GAIN + n * KC:V_GAIN + (n + 1) * KC], ALU.add, ALU.mult).then_inc(*mod_vec.up)
                        dve.tensor_scalar(vec[:, V_QKG:V_QKG + QCH], vec[:, V_QKG:V_QKG + QCH],
                                                     HEAD ** -0.5, None, ALU.mult).then_inc(*mod_vec.up)

        def norm_phase(n, hi=None, lo=None, plain=None):
            with ExitStack() as c:
                sq = [sb(f"sq{s}", [P, S], c=c) for s in range(2)]
                rs = sb("rs", [P, S], c=c)
                xn = [sb(f"xn{s}", [P, S], c=c) for s in range(2)]
                hf = [sb(f"hf{s}", [P, S], c=c) for s in range(2)] if plain is None else None
                sq_done, ms_step, ms_done = sig("sq_done"), sig("ms_step"), sig("ms_done")
                rt_done, rs_done, xn_done = sig("rt_done"), sig("rs_done"), sig("xn_done")
                h_done, h_hi, h_lo = sig("h_done"), sig("h_hi"), sig("h_lo")
                shift = (n // 2) * 6 * KC + 3 * (n % 2) * KC
                with nc.Block() as block:
                    @block.scalar
                    def _(act):
                        for k in range(KC):
                            if k >= 2:
                                act.wait_ge(*ms_step.at(k - 1))
                            act.activation(sq[k % 2][:, :], xt[:, k, :], ACT.Square).then_inc(*sq_done.up)
                        for h in range(NH):
                            act.wait_ge(*ms_done.at(h + 1))
                            act.activation(rs[:, h * HALF:(h + 1) * HALF], ps[:, h, :], ACT.Sqrt,
                                                      scale=1.0 / D, bias=con[:, C_EPS:C_EPS + 1]).then_inc(*rt_done.up)
                        if plain is None:
                            for k in range(KC):
                                act.wait_ge(*h_done.at(k + 1))
                                act.activation(hi[:, k, :], hf[k % 2][:, :], ACT.Copy).then_inc(*h_hi.up)

                    @block.tensor
                    def _(pe):
                        for k in range(KC):
                            pe.wait_ge(*sq_done.at(k + 1))
                            for h in range(NH):
                                ins = pe.matmul(ps[:, h, :], con[:, C_ONES:C_ONES + P],
                                                sq[k % 2][:, h * HALF:(h + 1) * HALF], start=k == 0, stop=k == KC - 1)
                                if k == KC - 1:
                                    ins.then_inc(*ms_done.up)
                            if k < KC - 1:
                                ins.then_inc(*ms_step.up)

                    @block.vector
                    def _(dve):
                        for h in range(NH):
                            dve.wait_ge(*rt_done.at(h + 1))
                            dve.reciprocal(rs[:, h * HALF:(h + 1) * HALF], rs[:, h * HALF:(h + 1) * HALF]).then_inc(*rs_done.up)
                        dve.wait_ge(*rs_done.at(NH))
                        for k in range(KC):
                            if k >= 2:
                                dve.wait_ge(*h_done.at(k - 1))
                            dve.tensor_tensor(xn[k % 2][:, :], xt[:, k, :], rs[:, :], ALU.mult).then_inc(*xn_done.up)
                            dve.wait_ge(*xn_done.at(k + 1))
                            if plain is None and k >= 2:
                                dve.wait_ge(*h_lo.at(k - 1))
                            out = plain[:, k, 1:S + 1] if plain is not None else hf[k % 2][:, :]
                            dve.tensor_scalar(out, xn[k % 2][:, :], gain[:, n * KC + k:n * KC + k + 1],
                                                        mod[:, shift + k:shift + k + 1], ALU.mult, ALU.add).then_inc(*h_done.up)

                    @block.gpsimd
                    def _(pool):
                        if plain is not None:
                            pool.memset(plain[:, :, 0:1], 0.0).then_inc(*h_lo.up)
                            return
                        for k in range(KC):
                            pool.wait_ge(*h_hi.at(k + 1))
                            pool.tensor_tensor(lo[:, k, :], hf[k % 2][:, :], hi[:, k, :].bitcast(F32),
                                                       ALU.subtract).then_inc(*h_lo.up)
                sq_done.passed(KC), ms_step.passed(KC - 1), ms_done.passed(NH), rt_done.passed(NH)
                rs_done.passed(NH), xn_done.passed(KC), h_done.passed(KC)
                h_hi.passed(KC if plain is None else 0)
                h_lo.passed(KC if plain is None else 1)

        def out_phase(w, src, gate, hi, lo):
            y_done, x_done = sig("y_done"), sig("x_done")
            with nc.Block() as block:
                @block.sync
                def _(sp):
                    with sp.Fori(0, KC // 2) as i:
                        for s in range(2):
                            load_weights(sp, w, s, i, src[bass.ds(2 * i + s, 1)].rearrange("a p k n -> (a p) k n"))

                @block.scalar
                def _(act):
                    with act.Fori(0, KC // 2) as i:
                        for s in range(2):
                            split_hi(act, w, s, i)

                @block.gpsimd
                def _(pool):
                    with pool.Fori(0, KC // 2) as i:
                        for s in range(2):
                            split_lo(pool, w, s, i)

                @block.tensor
                def _(pe):
                    with pe.Fori(0, KC // 2) as i:
                        for s in range(2):
                            pe.wait_ge(*w_lo_done[s].at(i + 1))
                            pe.wait_ge(*x_done.at(4 * i))
                            for h in range(NH):
                                hs = slice(h * HALF, (h + 1) * HALF)
                                ins = product(pe, ps[:, 2 * s + h, :], lambda k: w.hi[s][:, k, :],
                                              lambda k: w.lo[s][:, k, :], lambda k: hi[:, k, hs], lambda k: lo[:, k, hs])
                                ins.then_inc(*y_done.up) if h == 0 else None
                            ins.then_inc(*w_used[s].up)

                @block.vector
                def _(dve):
                    with dve.Fori(0, KC // 2) as i:
                        for s in range(2):
                            for h in range(NH):
                                if h == 0:
                                    dve.wait_ge(*y_done.at(2 * i + s + 1))
                                else:
                                    dve.wait_ge(*w_used[s].at(i + 1))
                                xs = xt[:, bass.ds(2 * i + s, 1), h * HALF:(h + 1) * HALF].rearrange("p a n -> p (a n)")
                                dve.scalar_tensor_tensor(xs, ps[:, 2 * s + h, :],
                                                                   mod[:, bass.ds(gate + 2 * i + s, 1)],
                                                                   xs, ALU.mult, ALU.add).then_inc(*x_done.up)
            slots_passed(KC // 2)
            y_done.passed(KC), x_done.passed(2 * KC)

        def rope_phase(cos, sin):
            with ExitStack() as c:
                pos = sb("pos", [P, S], I32, c)
                ang = sb("ang", [P, S], c=c)
                turns = sb("turns", [P, S], c=c)
                red = sb("red", [P, S], c=c)
                pos_in, ang_step, red_done, trig = sig("pos_in", 16), sig("ang_step"), sig("red_done"), sig("trig_done")
                with nc.Block() as block:
                    @block.sync
                    def _(sp):
                        sp.dma_start(pos[:, :], t["positions"]).then_inc(*pos_in.up)

                    @block.vector
                    def _(dve):
                        n = [0]

                        def step(ins):
                            ins.then_inc(*ang_step.up)
                            n[0] += 1
                            dve.wait_ge(*ang_step.at(n[0]))

                        dve.wait_ge(*pos_in.at(1))
                        step(dve.tensor_copy(ang[:, :], pos[:, :]))
                        step(dve.tensor_scalar(ang[:, :], ang[:, :], con[:, C_FREQ:C_FREQ + 1], None, ALU.mult))
                        for j, quarter in enumerate((0.0, 0.25)):
                            step(dve.tensor_scalar(turns[:, :], ang[:, :], 1.0 / TWO_PI, quarter, ALU.mult, ALU.add))
                            step(dve.tensor_scalar(turns[:, :], turns[:, :], ROUND, None, ALU.add))
                            step(dve.tensor_scalar(turns[:, :], turns[:, :], ROUND, None, ALU.subtract))
                            if j == 1:
                                dve.wait_ge(*trig.at(1))
                            step(dve.scalar_tensor_tensor(red[:, :], turns[:, :], -PI_A, ang[:, :], ALU.mult, ALU.add))
                            for part in (PI_B, PI_C):
                                step(dve.scalar_tensor_tensor(red[:, :], turns[:, :], -part, red[:, :], ALU.mult, ALU.add))
                            step(dve.tensor_scalar(red[:, :], red[:, :], quarter * TWO_PI, ANG_MAX, ALU.add, ALU.min))
                            dve.tensor_scalar(red[:, :], red[:, :], -ANG_MAX, None, ALU.max).then_inc(*red_done.up)
                        n_steps[0] = n[0]

                    @block.scalar
                    def _(act):
                        for j, out in enumerate((sin, cos)):
                            act.wait_ge(*red_done.at(j + 1))
                            act.activation(out[:, :], red[:, :], ACT.Sin).then_inc(*trig.up)
                pos_in.passed(1), ang_step.passed(n_steps[0]), red_done.passed(2), trig.passed(2)

        n_steps = [0]

        def qkv_phase(w, hi, lo, cos, sin, qk, vt):
            NQ = QCH + KCH
            with ExitStack() as c:
                raw = [sb(f"qk_raw{h}", [P, HALF], c=c) for h in range(NH)]
                sq = [sb(f"qk_sq{h}", [P, HALF], c=c) for h in range(NH)]
                rt = [sb(f"qk_rt{h}", [P, HALF], c=c) for h in range(NH)]
                m1 = [sb(f"qk_m1{h}", [P, HALF], c=c) for h in range(NH)]
                m2 = [sb(f"qk_m2{h}", [P, HALF], c=c) for h in range(NH)]
                main_done, sq_done, aux_done = sig("qk_main"), sig("qk_sq"), sig("qk_aux")
                rt_done, step_done, out_done = sig("qk_rt"), sig("qk_step"), sig("qk_out")
                v_done, v_out = sig("v_done"), sig("v_out")
                with nc.Block() as block:
                    @block.sync
                    def _(sp):
                        with sp.Fori(0, NQ // 2) as i:
                            for s in range(2):
                                load_weights(sp, w, s, i, t["wqk"][bass.ds(2 * i + s, 1)].rearrange("a p k n -> (a p) k n"))
                        for s in range(2):
                            load_weights(sp, w, s, NQ // 2, t["wv"][s])

                    @block.scalar
                    def _(act):
                        with act.Fori(0, NQ // 2) as i:
                            for s in range(2):
                                split_hi(act, w, s, i)
                            for u in range(4):
                                s, h = divmod(u, 2)
                                if h == 0:
                                    act.wait_ge(*main_done.at(2 * i + s + 1))
                                else:
                                    act.wait_ge(*w_used[s].at(i + 1))
                                act.wait_ge(*aux_done.at(4 * i + u - 1 if u >= 2 else 4 * i))
                                act.wait_ge(*out_done.at(4 * i + u - 1 if u >= 2 else 4 * i))
                                act.activation(sq[h][:, :], ps[:, u, :], ACT.Square)
                                act.activation(raw[h][:, :], ps[:, u, :], ACT.Copy,
                                                          scale=vec[:, bass.ds(V_QKG + 2 * i + s, 1)]).then_inc(*sq_done.up)
                                for v in ([u - 1] if u in (1, 2) else [2, 3] if u == 3 else []):
                                    act.wait_ge(*aux_done.at(4 * i + v + 1))
                                    act.activation(rt[v % 2][:, :], ps[:, 4 + v % 2, :], ACT.Sqrt,
                                                              scale=1.0 / HEAD, bias=con[:, C_EPS:C_EPS + 1]).then_inc(*rt_done.up)
                        for s in range(2):
                            split_hi(act, w, s, NQ // 2)

                    @block.gpsimd
                    def _(pool):
                        with pool.Fori(0, NQ // 2) as i:
                            for s in range(2):
                                split_lo(pool, w, s, i)
                        for s in range(2):
                            split_lo(pool, w, s, NQ // 2)

                    @block.tensor
                    def _(pe):
                        def aux(i, u):
                            h = u % 2
                            pe.wait_ge(*sq_done.at(4 * i + u + 1))
                            pe.wait_ge(*out_done.at(4 * i + u - 1 if u >= 2 else 4 * i))
                            pe.matmul(ps[:, 4 + h, :], con[:, C_BLOCK:C_BLOCK + P], sq[h][:, :], start=True, stop=True)
                            pe.matmul(ps[:, 6 + h, :], con[:, C_ROT:C_ROT + P], raw[h][:, :],
                                                  start=True, stop=True).then_inc(*aux_done.up)

                        with pe.Fori(0, NQ // 2) as i:
                            pe.wait_ge(*sq_done.at(4 * i))
                            for u in range(4):
                                s, h = divmod(u, 2)
                                if h == 0:
                                    pe.wait_ge(*w_lo_done[s].at(i + 1))
                                hs = slice(h * HALF, (h + 1) * HALF)
                                ins = product(pe, ps[:, u, :], lambda k: w.hi[s][:, k, :], lambda k: w.lo[s][:, k, :],
                                              lambda k: hi[:, k, hs], lambda k: lo[:, k, hs])
                                ins.then_inc(*(main_done if h == 0 else w_used[s]).up)
                                if u >= 1:
                                    aux(i, u - 1)
                            aux(i, 3)
                        pe.wait_ge(*sq_done.at(4 * (NQ // 2)))
                        for s in range(2):
                            pe.wait_ge(*w_lo_done[s].at(NQ // 2 + 1))
                            for b in range(2):
                                for q in range(NT // 2):
                                    tok = slice((b * 4 + q) * P, (b * 4 + q + 1) * P)
                                    ins = product(pe, ps[:, 2 * s + b, q * P:(q + 1) * P],
                                                  lambda k: hi[:, k, tok], lambda k: lo[:, k, tok],
                                                  lambda k: w.hi[s][:, k, :], lambda k: w.lo[s][:, k, :])
                                ins.then_inc(*v_done.up) if b == 0 else ins.then_inc(*w_used[s].up)

                    @block.vector
                    def _(dve):
                        with dve.Fori(0, NQ // 2) as i:
                            for u in range(4):
                                s, h = divmod(u, 2)
                                hs = slice(h * HALF, (h + 1) * HALF)
                                dve.wait_ge(*rt_done.at(4 * i + u + 1))
                                dve.reciprocal(rt[h][:, :], rt[h][:, :]).then_inc(*step_done.up)
                                dve.tensor_tensor(m1[h][:, :], raw[h][:, :], cos[:, hs], ALU.mult).then_inc(*step_done.up)
                                dve.tensor_tensor(m2[h][:, :], ps[:, 6 + h, :], sin[:, hs], ALU.mult).then_inc(*step_done.up)
                                dve.wait_ge(*step_done.at(16 * i + 4 * u + 3))
                                dve.tensor_tensor(m1[h][:, :], m1[h][:, :], m2[h][:, :], ALU.add).then_inc(*step_done.up)
                                dve.wait_ge(*step_done.at(16 * i + 4 * u + 4))
                                out = qk[:, bass.ds(2 * i + s, 1), hs].rearrange("p a n -> p (a n)")
                                dve.tensor_tensor(out, m1[h][:, :], rt[h][:, :], ALU.mult).then_inc(*out_done.up)
                        for s in range(2):
                            for b in range(2):
                                dve.wait_ge(*v_done.at(s + 1)) if b == 0 else dve.wait_ge(*w_used[s].at(NQ // 2 + 1))
                                dve.tensor_copy(vt[:, b * 4:b * 4 + 4, s * P:(s + 1) * P],
                                                         ps[:, 2 * s + b, :].rearrange("p (q n) -> p q n", q=4)).then_inc(*v_out.up)
                slots_passed(NQ // 2 + 1)
                n = 2 * NQ
                main_done.passed(NQ), sq_done.passed(n), aux_done.passed(n), rt_done.passed(n)
                step_done.passed(4 * n), out_done.passed(n), v_done.passed(2), v_out.passed(4)

        def attention_phase(qk, vt, hi, lo):
            with ExitStack() as c:
                qs = sb("qs", [P, QCH, P], c=c)
                ks = sb("ks", [P, KCH, BAND], c=c)
                vs = sb("vs", [P, 2, VDIM], c=c)
                sc = [sb(f"sc{b}", [P, GROUP, BAND], c=c) for b in range(2)]
                pb = [sb(f"pb{b}", [P, GROUP, 2 * P], c=c) for b in range(2)]
                pt = [sb(f"pt{b}", [P, GROUP * P], c=c) for b in range(2)]
                mx = sb("mx", [P, 4, GROUP], c=c)
                nm = sb("nm", [P, 4, GROUP], c=c)
                es = sb("es", [P, 4, GROUP], c=c)
                den = sb("den", [P, 4, GROUP], c=c)
                q_staged, v_staged, zeroed = sig("q_staged"), sig("v_staged"), sig("pb_zeroed")
                sc_done, tp_done, pv_done = sig("sc_done"), sig("tp_done"), sig("pv_done")
                a_step, nm_done, exp_done, b_step = sig("a_step"), sig("nm_done"), sig("exp_done"), sig("b_step")
                p_done, cur_out, prev_out, o_hi, o_lo = (sig("p_done"), sig("cur_out"), sig("prev_out"),
                                                         sig("o_hi"), sig("o_lo"))

                def tile_loop(eng, body):
                    body(0, True)
                    with eng.Fori(1, NT) as p:
                        body(p, False)

                def span(first):
                    return slice(CHUNK, BAND) if first else slice(0, BAND)

                with nc.Block() as block:
                    @block.gpsimd
                    def _(pool):
                        for b in range(2):
                            pool.memset(pb[b][:, :, 0:CHUNK], 0.0).then_inc(*zeroed.up)

                        def body(p, first):
                            if not first:
                                pool.wait_ge(*sc_done.at(4 * p))
                            pool.tensor_copy(qs[:, :, :], qk[:, 0:QCH, bass.ds(p * P, P)])
                            if first:
                                pool.tensor_copy(ks[:, :, CHUNK:BAND], qk[:, QCH:QCH + KCH, 0:P]).then_inc(*q_staged.up)
                            else:
                                pool.tensor_copy(ks[:, :, :], qk[:, QCH:QCH + KCH, bass.ds(p * P - CHUNK, BAND)]).then_inc(*q_staged.up)
                                pool.wait_ge(*pv_done.at(4 * p))
                            if first:
                                pool.tensor_copy(vs[:, 1, :], vt[:, 0, :]).then_inc(*v_staged.up)
                            else:
                                pool.tensor_copy(vs[:, :, :], vt[:, bass.ds(p - 1, 2), :]).then_inc(*v_staged.up)

                        tile_loop(pool, body)

                    @block.tensor
                    def _(pe):
                        def body(p, first):
                            def scores(g):
                                a, s = divmod(g, 2)
                                half = slice(s * HEAD, (s + 1) * HEAD)
                                if g >= 2 or not first:
                                    pe.wait_ge(*nm_done.at(4 * p + g - 1 if g >= 2 else 4 * p))
                                for j in range(GROUP):
                                    off = (j % 2) * BAND
                                    ins = pe.matmul(ps[:, 2 * s + j // 2, off + span(first).start:off + BAND],
                                                    qs[half, a * GROUP + j, :], ks[half, a, span(first)],
                                                    start=True, stop=True)
                                ins.then_inc(*sc_done.up)

                            pe.wait_ge(*q_staged.at(p + 1))
                            scores(0), scores(1)
                            for g in range(4):
                                a, s = divmod(g, 2)
                                pe.wait_ge(*p_done.at(4 * p + g + 1))
                                if g or not first:
                                    pe.wait_ge(*cur_out.at(4 * p + g))
                                if not first:
                                    pe.wait_ge(*prev_out.at(4 * (p - 1) + g))
                                for half in ((1,) if first else (0, 1)):
                                    for j in range(GROUP):
                                        ins = pe.transpose(ps[:, 4 + half, j * P:(j + 1) * P],
                                                           pb[g % 2][:, j, half * P:(half + 1) * P],
                                                           con[:, C_IDENT:C_IDENT + P])
                                ins.then_inc(*tp_done.up)
                                if g < 2:
                                    scores(g + 2)
                                if g == 0:
                                    pe.wait_ge(*v_staged.at(p + 1))
                                if s == 0 and not first:
                                    pe.wait_ge(*o_lo.at(2 * p))
                                pe.wait_ge(*cur_out.at(4 * p + g + 1))
                                if not first:
                                    pe.wait_ge(*prev_out.at(4 * (p - 1) + g + 1))
                                for half in ((1,) if first else (0, 1)):
                                    kv = (2 * a + s) * HEAD
                                    ins = pe.matmul(ps[s * HEAD:(s + 1) * HEAD, 6 + a, :],
                                                    vs[:, half, kv:kv + HEAD], pt[half][:, :],
                                                    start=half == 1 if first else half == 0, stop=half == 1)
                                ins.then_inc(*pv_done.up)

                        tile_loop(pe, body)

                    @block.vector
                    def _(dve):
                        def body(p, first):
                            mask = con[:, C_BAND + span(first).start:C_BAND + BAND]
                            n = BAND - span(first).start

                            def maximum(g):
                                s = g % 2
                                dve.wait_ge(*sc_done.at(4 * p + g + 1))
                                if g >= 2 or not first:
                                    dve.wait_ge(*exp_done.at(4 * p + g - 1 if g >= 2 else 4 * p))
                                for b in range(2):
                                    src = ps[:, 2 * s + b, 0:2 * BAND].rearrange("p (j n) -> p j n", j=2)[:, :, span(first)]
                                    dve.tensor_tensor(sc[s][:, 2 * b:2 * b + 2, span(first)], src,
                                                                mask.unsqueeze(1).to_broadcast([P, 2, n]), ALU.add).then_inc(*a_step.up)
                                dve.wait_ge(*a_step.at(16 * p + 4 * g + 2))
                                dve.tensor_reduce(mx[:, g, :], sc[s][:, :, span(first)], AX.X, ALU.max).then_inc(*a_step.up)
                                dve.wait_ge(*a_step.at(16 * p + 4 * g + 3))
                                sink = vec[:, V_SINK + 4 * g:V_SINK + 4 * g + 4]
                                dve.tensor_tensor(mx[:, g, :], mx[:, g, :], sink, ALU.max).then_inc(*a_step.up)
                                dve.wait_ge(*a_step.at(16 * p + 4 * g + 4))
                                dve.tensor_tensor(es[:, g, :], sink, mx[:, g, :], ALU.subtract)
                                dve.tensor_scalar(nm[:, g, :], mx[:, g, :], -1.0, None, ALU.mult).then_inc(*nm_done.up)

                            def normalise(g):
                                dve.wait_ge(*exp_done.at(4 * p + g + 1))
                                dve.tensor_tensor(den[:, g, :], den[:, g, :], es[:, g, :], ALU.add).then_inc(*b_step.up)
                                dve.wait_ge(*b_step.at(8 * p + 2 * g + 1))
                                dve.reciprocal(den[:, g, :], den[:, g, :]).then_inc(*b_step.up)
                                dve.wait_ge(*b_step.at(8 * p + 2 * g + 2))
                                pv = pb[g % 2][:, :, CHUNK + span(first).start:2 * P]
                                dve.tensor_tensor(pv, pv, den[:, g, :].unsqueeze(2).to_broadcast([P, GROUP, n]),
                                                            ALU.mult).then_inc(*p_done.up)

                            def take_current(g):
                                dve.wait_ge(*tp_done.at(4 * p + g + 1))
                                if g or not first:
                                    dve.wait_ge(*pv_done.at(4 * p + g))
                                dve.tensor_copy(pt[1][:, :], ps[:, 5, :]).then_inc(*cur_out.up)

                            def low_part(a):
                                dve.wait_ge(*o_hi.at(2 * p + a + 1))
                                tok = bass.ds(p * P, P)
                                dve.tensor_tensor(lo[:, a * GROUP:(a + 1) * GROUP, tok],
                                                          ps[:, 6 + a, :].rearrange("p (j n) -> p j n", j=GROUP),
                                                          hi[:, a * GROUP:(a + 1) * GROUP, tok].bitcast(F32), ALU.subtract).then_inc(*o_lo.up)

                            maximum(0), maximum(1), normalise(0)
                            take_current(0), maximum(2), normalise(1)
                            take_current(1), maximum(3), normalise(2)
                            take_current(2), low_part(0), normalise(3)
                            take_current(3), low_part(1)

                        tile_loop(dve, body)

                    @block.scalar
                    def _(act):
                        def body(p, first):
                            if first:
                                act.wait_ge(*zeroed.at(2))

                            def exponentials(g):
                                act.wait_ge(*nm_done.at(4 * p + g + 1))
                                if g >= 2 or not first:
                                    act.wait_ge(*tp_done.at(4 * p + g - 1 if g >= 2 else 4 * p))
                                for j in range(GROUP):
                                    act.activation(pb[g % 2][:, j, CHUNK + span(first).start:2 * P], sc[g % 2][:, j, span(first)],
                                                   ACT.Exp, bias=nm[:, g, j:j + 1],
                                                   accum_out=den[:, g, j:j + 1])
                                act.activation(es[:, g, :], es[:, g, :], ACT.Exp).then_inc(*exp_done.up)

                            def take_previous(g):
                                if first:
                                    return
                                act.wait_ge(*tp_done.at(4 * p + g + 1))
                                act.wait_ge(*pv_done.at(4 * p + g))
                                act.activation(pt[0][:, :], ps[:, 4, :], ACT.Copy).then_inc(*prev_out.up)

                            def high_part(a):
                                act.wait_ge(*pv_done.at(4 * p + 2 * a + 2))
                                settle(act)
                                act.activation(hi[:, a * GROUP:(a + 1) * GROUP, bass.ds(p * P, P)],
                                                       ps[:, 6 + a, :].rearrange("p (j n) -> p j n", j=GROUP), ACT.Copy).then_inc(*o_hi.up)

                            exponentials(0), exponentials(1)
                            take_previous(0), exponentials(2)
                            take_previous(1), exponentials(3)
                            take_previous(2), high_part(0)
                            take_previous(3), high_part(1)

                        tile_loop(act, body)
                q_staged.passed(NT), v_staged.passed(NT), zeroed.passed(2)
                for x in (sc_done, tp_done, pv_done, nm_done, exp_done, p_done, cur_out):
                    x.passed(4 * NT)
                prev_out.passed(4 * (NT - 1))
                a_step.passed(16 * NT), b_step.passed(8 * NT), o_hi.passed(2 * NT), o_lo.passed(2 * NT)

        def ffn_phase(layer, hi, lo):
            with ExitStack() as c:
                w1 = [sb(f"w1_raw{f}", [P, KC, 2 * P], c=c) for f in range(FS)]
                w1h = [sb(f"w1_hi{f}", [P, KC, 2 * P], F32R, c) for f in range(FS)]
                w1l = [sb(f"w1_lo{f}", [P, KC, 2 * P], F32R, c) for f in range(FS)]
                w2 = sb("w2_raw", [P, FS, D], c=c)
                w2h, w2l = sb("w2_hi", [P, FS, D], F32R, c), sb("w2_lo", [P, FS, D], F32R, c)
                ah, al = sb("act_hi", [P, FS, S], F32R, c), sb("act_lo", [P, FS, S], F32R, c)
                sg = [sb(f"silu{b}", [P, HALF], c=c) for b in range(2)]
                af = [sb(f"act{b}", [P, HALF], c=c) for b in range(2)]
                w1_in = [sig(f"w1_in{f}", 16) for f in range(FS)]
                w1_hi = [sig(f"w1_hi_done{f}") for f in range(FS)]
                w1_lo = [sig(f"w1_lo_done{f}") for f in range(FS)]
                w2_in, w2_hi, w2_lo, w2_used = sig("w2_in", 16), sig("w2_hi_done"), sig("w2_lo_done"), sig("w2_used")
                up_done, silu_done, act_step, act_done = sig("up_done"), sig("silu_done"), sig("act_step"), sig("act_done")
                y_done, x_done = sig("ffn_y"), sig("ffn_x")
                win, wout = t["ffn_w_in"], t["ffn_w_out"]

                with nc.Block() as block:
                    @block.sync
                    def _(sp):
                        def load_in(i, f):
                            sp.wait_ge(*w1_lo[f].at(i))
                            settle(sp)
                            sp.dma_start(w1[f][:, :, :], win[bass.ds((layer * FITER + i) * FS + f, 1)]
                                                     .rearrange("a p k n -> (a p) k n")).then_inc(*w1_in[f].up)

                        def load_out(i):
                            sp.wait_ge(*w2_lo.at(i))
                            settle(sp)
                            sp.dma_start(w2[:, :, :], wout[bass.ds(layer * FITER + i, 1)]
                                                  .rearrange("a p f n -> (a p) f n")).then_inc(*w2_in.up)

                        with sp.Fori(0, FITER) as i:
                            load_in(i, 0), load_in(i, 1), load_out(i)

                    def split_in_hi(act, i, f, prior=None):
                        act.wait_ge(*w1_in[f].at(i + 1))
                        if prior is not None:
                            act.wait_ge(*up_done.at(prior))
                        act.activation(w1h[f][:, :, :], w1[f][:, :, :], ACT.Copy).then_inc(*w1_hi[f].up)

                    def split_in_lo(pool, i, f):
                        pool.wait_ge(*w1_hi[f].at(i + 1))
                        pool.tensor_tensor(w1l[f][:, :, :], w1[f][:, :, :], w1h[f][:, :, :].bitcast(F32),
                                                       ALU.subtract).then_inc(*w1_lo[f].up)

                    @block.scalar
                    def _(act):
                        def silu(i, q):
                            act.wait_ge(*up_done.at(4 * i + q + 1))
                            act.wait_ge(*act_done.at(4 * i + q - 1 if q >= 2 else 4 * i))
                            act.activation(sg[q % 2][:, :], ps[:, 2 * (q % 2), :], ACT.Silu).then_inc(*silu_done.up)

                        def step(i, last):
                            silu(i, 0)
                            act.wait_ge(*w2_in.at(i + 1))
                            act.wait_ge(*w2_used.at(i))
                            act.activation(w2h[:, :, :], w2[:, :, :], ACT.Copy).then_inc(*w2_hi.up)
                            silu(i, 1), silu(i, 2)
                            if not last:
                                split_in_hi(act, i + 1, 0, 4 * i + 3)
                            silu(i, 3)
                            if not last:
                                split_in_hi(act, i + 1, 1, 4 * i + 4)

                        split_in_hi(act, 0, 0), split_in_hi(act, 0, 1)
                        with act.Fori(0, FITER - 1) as i:
                            step(i, False)
                        step(FITER - 1, True)

                    @block.gpsimd
                    def _(pool):
                        def out_lo(i):
                            pool.wait_ge(*w2_hi.at(i + 1))
                            pool.tensor_tensor(w2l[:, :, :], w2[:, :, :], w2h[:, :, :].bitcast(F32), ALU.subtract).then_inc(*w2_lo.up)

                        split_in_lo(pool, 0, 0), split_in_lo(pool, 0, 1)
                        with pool.Fori(0, FITER - 1) as i:
                            out_lo(i), split_in_lo(pool, i + 1, 0), split_in_lo(pool, i + 1, 1)
                        out_lo(FITER - 1)

                    @block.tensor
                    def _(pe):
                        with pe.Fori(0, FITER) as i:
                            for q in range(4):
                                h, f = divmod(q, 2)
                                hs = slice(h * HALF, (h + 1) * HALF)
                                if h == 0:
                                    pe.wait_ge(*w1_lo[f].at(i + 1))
                                pe.wait_ge(*act_done.at(4 * i + q - 1 if q >= 2 else 4 * i))
                                for g in range(2):
                                    gs = slice(g * P, (g + 1) * P)
                                    ins = product(pe, ps[:, 2 * f + g, :], lambda k: w1h[f][:, k, gs],
                                                  lambda k: w1l[f][:, k, gs], lambda k: hi[:, k, hs], lambda k: lo[:, k, hs])
                                ins.then_inc(*up_done.up)
                            for r in range(2 * KC):
                                h, d = divmod(r, KC)
                                hs = slice(h * HALF, (h + 1) * HALF)
                                ds = slice(d * P, (d + 1) * P)
                                if r == 0:
                                    pe.wait_ge(*w2_lo.at(i + 1))
                                if d == 0:
                                    pe.wait_ge(*act_done.at(4 * i + 2 * h + 2))
                                pe.wait_ge(*x_done.at(16 * i + r - 3 if r >= 4 else 16 * i))
                                ins = product(pe, ps[:, 4 + r % 4, :], lambda k: w2h[:, k, ds], lambda k: w2l[:, k, ds],
                                              lambda k: ah[:, k, hs], lambda k: al[:, k, hs], kc=FS)
                                ins.then_inc(*(y_done if r < 2 * KC - 1 else w2_used).up)

                    @block.vector
                    def _(dve):
                        with dve.Fori(0, FITER) as i:
                            for q in range(4):
                                h, f = divmod(q, 2)
                                hs = slice(h * HALF, (h + 1) * HALF)
                                dve.wait_ge(*silu_done.at(4 * i + q + 1))
                                dve.tensor_tensor(af[f][:, :], ps[:, 2 * f + 1, :], sg[f][:, :], ALU.mult).then_inc(*act_step.up)
                                dve.wait_ge(*act_step.at(8 * i + 2 * q + 1))
                                dve.tensor_copy(ah[:, f, hs], af[f][:, :]).then_inc(*act_step.up)
                                dve.wait_ge(*act_step.at(8 * i + 2 * q + 2))
                                dve.tensor_tensor(al[:, f, hs], af[f][:, :], ah[:, f, hs].bitcast(F32),
                                                              ALU.subtract).then_inc(*act_done.up)
                            for r in range(2 * KC):
                                h, d = divmod(r, KC)
                                xs = xt[:, d, h * HALF:(h + 1) * HALF]
                                if r < 2 * KC - 1:
                                    dve.wait_ge(*y_done.at((2 * KC - 1) * i + r + 1))
                                else:
                                    dve.wait_ge(*w2_used.at(i + 1))
                                g = (layer * 6 + 5) * KC + d
                                dve.scalar_tensor_tensor(xs, ps[:, 4 + r % 4, :], mod[:, g:g + 1], xs,
                                                                   ALU.mult, ALU.add).then_inc(*x_done.up)
                for f in range(FS):
                    for x in (w1_in, w1_hi, w1_lo):
                        x[f].passed(FITER)
                for x in (w2_in, w2_hi, w2_lo, w2_used):
                    x.passed(FITER)
                for x in (up_done, silu_done, act_done):
                    x.passed(4 * FITER)
                act_step.passed(8 * FITER), y_done.passed((2 * KC - 1) * FITER), x_done.passed(2 * KC * FITER)

        def rwkv_projections():
            scr = t["scratch"]
            with ExitStack() as c:
                h = sb("h_prev", [P, KC, S + 1], c=c)
                norm_phase(2, plain=h)
                w = Weights(sb, c)
                xx = sb("xx", [P, KC, S], c=c)
                mh = [sb(f"mix_hi{b}", [P, KC, HALF], F32R, c) for b in range(NH)]
                ml = [sb(f"mix_lo{b}", [P, KC, HALF], F32R, c) for b in range(NH)]
                with ExitStack() as c2:
                    mf = [sb(f"mix{b}", [P, HALF], c=c2) for b in range(2)]
                    stage = [sb(f"stage{b}", [P, HALF], c=c2) for b in range(2)]
                    tf, th, tl = sb("lora", [P, HALF], c=c2), sb("lora_hi", [P, HALF], F32R, c2), sb("lora_lo", [P, HALF], F32R, c2)
                    xx_done, mix_f, mix_h, mix_l = sig("xx_done"), sig("mix_f"), sig("mix_hi"), sig("mix_lo")
                    taken = [sig(f"taken{s}") for s in range(2)]
                    stored = [sig(f"stored{s}", 16) for s in range(2)]
                    lo1_done, lo1_act, lo1_step, lo1_lo = sig("lora1_done"), sig("lora1_act"), sig("lora1_step"), sig("lora1_lo")
                    lo2_done = sig("lora2_done")
                    NCH = 2 * 3 * KC // 2

                    def scratch_of(a, half, j):
                        return scr[a, half * 8:(half + 1) * 8, :, j, :].rearrange("c p n -> p c n")

                    def mix_make(dve, n, half, mix, k):
                        m = KC * n + k
                        if isinstance(m, int) and m < 2:
                            pass
                        else:
                            dve.wait_ge(*mix_l.at(m - 1))
                        hs = slice(half * HALF, (half + 1) * HALF)
                        kk = k if isinstance(k, int) else None
                        ks = slice(k, k + 1) if kk is not None else bass.ds(k, 1)
                        dve.scalar_tensor_tensor(
                            mf_of(k)[:, :], xx[:, ks, hs].rearrange("p a n -> p (a n)"),
                            vec[:, bass.ds(V_MU + mix * KC + k, 1)],
                            h[:, ks, half * HALF + 1:(half + 1) * HALF + 1].rearrange("p a n -> p (a n)"), ALU.mult, ALU.add).then_inc(*mix_f.up)

                    slot = [0]

                    def mf_of(k):
                        return mf[k % 2] if isinstance(k, int) else mf[slot[0]]

                    def one(buf, k):
                        return buf[:, bass.ds(k, 1), :].rearrange("p a n -> p (a n)")

                    def mix_high(act, n, half, k):
                        act.wait_ge(*mix_f.at(KC * n + k + 1))
                        settle(act)
                        act.activation(one(mh[half], k), mf_of(k)[:, :], ACT.Copy).then_inc(*mix_h.up)

                    def mix_low(pool, n, half, k):
                        pool.wait_ge(*mix_h.at(KC * n + k + 1))
                        pool.tensor_tensor(one(ml[half], k), mf_of(k)[:, :], one(mh[half], k).bitcast(F32),
                                                    ALU.subtract).then_inc(*mix_l.up)

                    def rkv_loop(eng, body):
                        with eng.Fori(0, 3) as p:
                            for half in range(NH):
                                with eng.Fori(0, KC // 2) as cc:
                                    for s in range(2):
                                        slot[0] = s
                                        body(p, half, cc, s, 4 * (2 * p + half) + cc, 2 * p + half)

                    with nc.Block() as block:
                        @block.sync
                        def _(sp):
                            rkv_loop(sp, lambda p, half, cc, s, i, n: load_weights(
                                sp, w, s, i, t["w_rkv"][bass.ds(p * KC + 2 * cc + s, 1)].rearrange("a p k n -> (a p) k n")))
                            for l in range(3):
                                load_weights(sp, w, 0, NCH + l, t["lora1"][l])
                                load_weights(sp, w, 1, NCH + l, t["lora2"][l])

                        def split_hi_dve(dve, s, i):
                            dve.wait_ge(*w_loaded[s].at(i + 1))
                            dve.wait_ge(*w_used[s].at(i))
                            dve.tensor_copy(w.hi[s][:, :, :], w.raw[s][:, :, :]).then_inc(*w_hi_done[s].up)

                        @block.vector
                        def _(dve):
                            for k in range(KC):
                                dve.tensor_tensor(xx[:, k, :], h[:, k, 0:S], h[:, k, 1:S + 1], ALU.subtract).then_inc(*xx_done.up)
                            dve.wait_ge(*xx_done.at(KC))
                            for k in range(KC):
                                mix_make(dve, 0, 0, 0, k)

                            def body(p, half, cc, s, i, n):
                                split_hi_dve(dve, s, i)
                                mix_make(dve, n + 1, 1 - half, p + half, 2 * cc + s)
                            rkv_loop(dve, body)
                            for l in range(3):
                                split_hi_dve(dve, 0, NCH + l)
                                split_hi_dve(dve, 1, NCH + l)
                                for half in range(NH):
                                    n = 6 + 2 * l + half
                                    if n < 11:
                                        for k in range(KC):
                                            mix_make(dve, n + 1, 1 - half, 3 + l + half, k)
                                    dve.wait_ge(*lo1_act.at(n - 5))
                                    dve.tensor_copy(th[:, :], tf[:, :]).then_inc(*lo1_step.up)
                                    dve.wait_ge(*lo1_step.at(n - 5))
                                    dve.tensor_tensor(tl[:, :], tf[:, :], th[:, :].bitcast(F32), ALU.subtract).then_inc(*lo1_lo.up)

                        @block.gpsimd
                        def _(pool):
                            for k in range(KC):
                                mix_low(pool, 0, 0, k)

                            def body(p, half, cc, s, i, n):
                                split_lo(pool, w, s, i)
                                mix_low(pool, n + 1, 1 - half, 2 * cc + s)
                            rkv_loop(pool, body)
                            for l in range(3):
                                split_lo(pool, w, 0, NCH + l)
                                split_lo(pool, w, 1, NCH + l)
                                for half in range(NH):
                                    n = 6 + 2 * l + half
                                    if n < 11:
                                        for k in range(KC):
                                            mix_low(pool, n + 1, 1 - half, k)

                        @block.scalar
                        def _(act):
                            for k in range(KC):
                                mix_high(act, 0, 0, k)

                            def take(src, s, i, func, bias, dst):
                                act.wait_ge(*stored[s].at(i))
                                act.activation(stage[s][:, :], src, func, bias=bias).then_inc(*taken[s].up)
                                act.wait_ge(*taken[s].at(i + 1))
                                settle(act)
                                act.dma_start(dst, stage[s][:, :].rearrange("p (c n) -> p c n", n=CHUNK)).then_inc(*stored[s].up)

                            def body(p, half, cc, s, i, n):
                                act.wait_ge(*w_used[1].at(4 * n))
                                mix_high(act, n + 1, 1 - half, 2 * cc + s)
                                act.wait_ge(*w_used[s].at(i + 1))
                                dst = scr[bass.ds(p, 1), half * 8:(half + 1) * 8, :, bass.ds(2 * cc + s, 1), :]
                                take(ps[:, s, :], s, i, ACT.Copy, 0.0, dst.rearrange("b c p a n -> p (b c) (a n)"))
                            rkv_loop(act, body)
                            act.wait_ge(*w_used[1].at(NCH))
                            for l, func in enumerate((ACT.Tanh, ACT.Copy, ACT.Sigmoid)):
                                for half in range(NH):
                                    n = 6 + 2 * l + half
                                    act.wait_ge(*lo1_done.at(n - 5))
                                    if n > 6:
                                        act.wait_ge(*lo2_done.at((n - 6) * KC))
                                    act.activation(tf[:, :], ps[:, 2 + half, :], func).then_inc(*lo1_act.up)
                                    if n < 11:
                                        for k in range(KC):
                                            mix_high(act, n + 1, 1 - half, k)
                                    for j in range(KC):
                                        act.wait_ge(*lo2_done.at((n - 6) * KC + j + 1))
                                        col = (V_W0, V_A0, None)[l]
                                        take(ps[:, 4 + j % 2, :], j % 2, NCH + (n - 6) * 4 + j // 2,
                                             ACT.Sigmoid if l < 2 else ACT.Copy,
                                             vec[:, col + j:col + j + 1] if l < 2 else 0.0, scratch_of(3 + l, half, j))
                            for s in range(2):
                                act.wait_ge(*stored[s].at(NCH + 24))

                        @block.tensor
                        def _(pe):
                            def body(p, half, cc, s, i, n):
                                pe.wait_ge(*w_lo_done[s].at(i + 1))
                                pe.wait_ge(*mix_l.at(KC * n + KC))
                                pe.wait_ge(*taken[s].at(i))
                                product(pe, ps[:, s, :], lambda k: w.hi[s][:, k, :], lambda k: w.lo[s][:, k, :],
                                                     lambda k: mh[half][:, k, :], lambda k: ml[half][:, k, :]).then_inc(*w_used[s].up)
                            rkv_loop(pe, body)
                            for l in range(3):
                                pe.wait_ge(*w_lo_done[0].at(NCH + l + 1))
                                pe.wait_ge(*w_lo_done[1].at(NCH + l + 1))
                                for half in range(NH):
                                    n = 6 + 2 * l + half
                                    pe.wait_ge(*mix_l.at(KC * n + KC))
                                    if n > 7:
                                        pe.wait_ge(*lo1_act.at(n - 7))
                                    product(pe, ps[:, 2 + half, :], lambda k: w.hi[0][:, k, :],
                                                        lambda k: w.lo[0][:, k, :], lambda k: mh[half][:, k, :],
                                                        lambda k: ml[half][:, k, :]).then_inc(*lo1_done.up)
                                    pe.wait_ge(*lo1_lo.at(n - 5))
                                    for j in range(KC):
                                        if n > 6 or j >= 2:
                                            pe.wait_ge(*taken[j % 2].at(NCH + (n - 6) * 4 + j // 2))
                                        product(pe, ps[:, 4 + j % 2, :], lambda k: w.hi[1][:, j, :],
                                                            lambda k: w.lo[1][:, j, :], lambda k: th[:, :],
                                                            lambda k: tl[:, :], kc=1).then_inc(*lo2_done.up)
                                for s in range(2):
                                    pe.matmul(ps[:, 6, 0:1], con[:, C_IDENT:C_IDENT + P], con[:, 0:1],
                                                           start=True, stop=True).then_inc(*w_used[s].up)
                    slots_passed(NCH + 3)
                    xx_done.passed(KC), mix_f.passed(12 * KC), mix_h.passed(12 * KC), mix_l.passed(12 * KC)
                    for s in range(2):
                        taken[s].passed(NCH + 24), stored[s].passed(NCH + 24)
                    for x in (lo1_done, lo1_act, lo1_step, lo1_lo):
                        x.passed(6)
                    lo2_done.passed(6 * KC)

        def wkv_phase():
            scr, zscr = t["scratch"], t["z_scratch"]
            NC = S // CHUNK
            W8 = [P, PAIRS, CHUNK]
            with ExitStack() as c:
                def st(name):
                    return sb(name, W8, c=c)

                def bd(name):
                    x = sb(name, [P, PAIRS, P], c=c)
                    diagonals.append(x)
                    return x

                diagonals = []
                rt, kt_, vt_, st_, at_ = st("r"), st("k"), st("v"), st("decay_sig"), st("a")
                vbd = bd("v_bd")
                kk, rn, k2, lcum, lprev = st("kk"), st("rn"), st("k2"), st("lcum"), st("lprev")
                ep, em, eq, bb, rk, sq = st("e_pos"), st("e_neg"), st("e_prev"), st("b"), st("rk"), st("kk_sq")
                ar = sb("ar", [P, PAIRS, 2, CHUNK], c=c)
                bbd, kbd, ntbd = bd("b_bd"), bd("k_bd"), bd("n_t")
                ntm = [sb(f"n_t_level{b}", [P, PAIRS, P], c=c) for b in range(2)]
                wbd, tbd = bd("one_plus_x"), bd("inv")
                abd, rbd = [bd(f"a_bd{b}") for b in range(2)], [bd(f"r_bd{b}") for b in range(2)]
                aak, arb, ark = ([bd(f"{x}{b}") for b in range(2)] for x in ("a_k", "r_b", "r_k"))
                inv = [bd(f"inv_t_bd{b}") for b in range(2)]
                btok, ktok = [bd(f"b_tok{b}") for b in range(2)], [bd(f"k_tok{b}") for b in range(2)]
                vtok, gt, bonus = ([st(f"{x}{b}") for b in range(2)] for x in ("v_tok", "gate", "bonus"))
                pend = [sb(f"p_end{b}", [P, PAIRS], c=c) for b in range(2)]
                state, xst, ust = st("state"), st("x_st"), st("u_st")
                yc, ysq, ybd, z, bias = st("y_centred"), st("y_sq"), bd("y_bd"), st("z"), st("bias")
                mean, var = sb("mean", [P, PAIRS], c=c), sb("var", [P, PAIRS], c=c)
                reset, reset_in = sb("reset", [P, HALF], c=c), sig("reset_in", 16)
                DEC = math.exp(-0.5)

                names = ("tiles_in v_in kk_done t1_done l_done mx_done rn_done ar_done bb_done kb_done bonus_done nt_done "
                         "arb_done g_out sq_done_w ss_done rt_done_w e_done eq_done pend_done bd_done v_tok b_tok k_tok v_out "
                         "b_out k_out ka_step k2_done lq_done kkn_done b_done rk_step rk_done bonus_ps g1_done g2_done "
                         "lev_mask inv_one x_done_w w_done tr_done t_done xs_done xe_done us_done ue_done s_step s_done y_done_w "
                         "m_step yc_done ysq_done var_done yrt_done yrn_done ybd_done yf_done z1_done bias_done z_step "
                         "zeros").split()
                g = {n: sig("wkv_" + n, 16 if n in ("tiles_in", "v_in") else 1) for n in names}
                g_in = [sig(f"g_in{b}", 16) for b in range(2)]
                chunk_used = [sig(f"chunk_used{b}") for b in range(2)]
                post_done = [sig(f"post_done{b}") for b in range(2)]
                z_stored = sig("z_stored", 16)
                idst, ident = con[:, C_IDST:C_IDST + CHUNK], con[:, C_IDENT:C_IDENT + P]

                def flat(x):
                    return x.rearrange("p a n -> p (a n)")

                def per_pair(cols):
                    return cols.unsqueeze(2).to_broadcast(W8)

                def column(v):
                    return per_pair(vec[:, v:v + PAIRS])

                def bank(b, j0=0, j1=PAIRS):
                    return ps[:, b, j0 * CHUNK:j1 * CHUNK].rearrange("p (a n) -> p a n", n=CHUNK)

                def group(b):
                    return ps[:, b, :].rearrange("p (a n) -> p a n", n=P)

                def halves(x, pairs=slice(0, PAIRS)):
                    return [(slice(h * HEAD, (h + 1) * HEAD), x[h * HEAD:(h + 1) * HEAD, pairs, h * HEAD:(h + 1) * HEAD])
                            for h in range(2)]

                QP = PAIRS // 2
                NL = len(LEVELS)

                def periods(eng, first, period, last):
                    def at(c):
                        return (c, c // 2, c % 2) if 0 <= c < NC else None

                    first(at(0))
                    period(at(1), at(0), None)
                    with eng.Fori(0, NC // 2 - 2) as i:
                        period((2 * i + 2, i + 1, 0), (2 * i + 1, i, 1), (2 * i, i, 0))
                        period((2 * i + 3, i + 1, 1), (2 * i + 2, i + 1, 0), (2 * i + 1, i, 1))
                    for c in range(NC - 3, NC):
                        period(at(c + 1), at(c), at(c - 1))
                    last(at(NC - 1))

                with nc.Block() as block:
                    @block.sync
                    def _(sp):
                        sp.dma_start(reset[:, :], t["consts"][:, C_RESET:C_ALL]).then_inc(*reset_in.up)
                        sp.wait_ge(*g["zeros"].at(1))

                        def load_tiles(ch):
                            sp.wait_ge(*g["rk_done"].at(ch))
                            sp.wait_ge(*g["ar_done"].at(2 * ch))
                            settle(sp)
                            for n, x in ((0, rt), (1, kt_), (3, st_), (4, at_)):
                                sp.dma_start(x[:, :, :], scr[n, bass.ds(ch, 1)].rearrange("c p a n -> (c p) a n")).then_inc(*g["tiles_in"].up)

                        def load_values(ch):
                            sp.wait_ge(*g["bonus_done"].at(ch))
                            settle(sp)
                            sp.dma_start(vt_[:, :, :], scr[2, bass.ds(ch, 1)].rearrange("c p a n -> (c p) a n")).then_inc(*g["v_in"].up)
                            for h in range(2):
                                hs = slice(h * HEAD, (h + 1) * HEAD)
                                sp.dma_start(vbd[hs, :, hs], scr[2, bass.ds(ch, 1), hs].rearrange("c p a n -> (c p) a n")).then_inc(*g["v_in"].up)

                        def load_gate(ch, i, b):
                            sp.wait_ge(*post_done[b].at(i))
                            settle(sp)
                            sp.dma_start(gt[b][:, :, :], scr[5, bass.ds(ch, 1)].rearrange("c p a n -> (c p) a n")).then_inc(*g_in[b].up)

                        def store_z(ch, i, b):
                            sp.wait_ge(*post_done[b].at(i + 1))
                            settle(sp)
                            sp.dma_start(zscr[bass.ds(ch, 1)].rearrange("c p a n -> (c p) a n"), z[:, :, :]).then_inc(*z_stored.up)

                        def first(x):
                            load_tiles(0), load_values(0), load_gate(*x)
                            load_tiles(1), load_values(1)

                        def period(x, y, zz):
                            if x is not None and not (isinstance(x[0], int) and x[0] == NC - 1):
                                load_tiles(x[0] + 1), load_values(x[0] + 1)
                            if zz is not None:
                                store_z(*zz)
                            if x is not None:
                                load_gate(*x)

                        periods(sp, first, period, lambda x: store_z(*x))
                        sp.wait_ge(*z_stored.at(NC))

                    @block.gpsimd
                    def _(pool):
                        for x in diagonals:
                            pool.memset(x[:, :, :], 0.0)
                        pool.memset(state[:, :, :], 0.0).then_inc(*g["zeros"].up)

                        def keys(ch):
                            pool.wait_ge(*g["t1_done"].at(ch + 1))
                            pool.tensor_tensor(k2[:, :, :], k2[:, :, :], column(V_KA), ALU.mult).then_inc(*g["ka_step"].up)
                            pool.wait_ge(*g["ka_step"].at(ch + 1))
                            pool.tensor_tensor(k2[:, :, :], k2[:, :, :], kt_[:, :, :], ALU.add).then_inc(*g["k2_done"].up)
                            pool.wait_ge(*g["l_done"].at(ch + 1))
                            pool.tensor_tensor(lprev[:, :, :], lcum[:, :, :], st_[:, :, :], ALU.subtract).then_inc(*g["lq_done"].up)

                        def normed_keys(ch):
                            pool.wait_ge(*g["rn_done"].at(ch + 1))
                            pool.tensor_tensor(kk[:, :, :], kk[:, :, :], rn[:, :, :], ALU.mult).then_inc(*g["kkn_done"].up)
                            pool.wait_ge(*g["kkn_done"].at(ch + 1))
                            pool.tensor_tensor(bb[:, :, :], kk[:, :, :], at_[:, :, :], ALU.mult).then_inc(*g["b_done"].up)

                        def bonus_terms(ch):
                            pool.wait_ge(*g["k2_done"].at(ch + 1))
                            pool.tensor_tensor(rk[:, :, :], rt[:, :, :], k2[:, :, :], ALU.mult).then_inc(*g["rk_step"].up)
                            pool.wait_ge(*g["rk_step"].at(ch + 1))
                            pool.tensor_tensor(rk[:, :, :], rk[:, :, :], column(V_RK), ALU.mult).then_inc(*g["rk_done"].up)

                        def level_mask(ch, l):
                            if l == 0:
                                pool.wait_ge(*g["nt_done"].at(ch + 1))
                            pool.wait_ge(*g["x_done_w"].at(2 * NL * ch + 2 * l - 2))
                            m = con[:, C_LEVEL + l * P:C_LEVEL + (l + 1) * P].unsqueeze(1).to_broadcast([P, PAIRS, P])
                            pool.tensor_tensor(ntm[l % 2][:, :, :], ntbd[:, :, :], m, ALU.mult).then_inc(*g["lev_mask"].up)

                        def first_inverse(ch, i, b):
                            pool.wait_ge(*g["lev_mask"].at(NL * ch + 1))
                            pool.wait_ge(*chunk_used[b].at(i))
                            pool.tensor_tensor(inv[b][:, :, :], ntm[0][:, :, :], ident.unsqueeze(1).to_broadcast([P, PAIRS, P]),
                                               ALU.add).then_inc(*g["inv_one"].up)

                        def bonus_and_bias(ch, i, b):
                            pool.wait_ge(*g["bonus_done"].at(ch + 1))
                            pool.tensor_tensor(bias[:, :, :], bonus[b][:, :, :], column(V_LNB), ALU.add).then_inc(*g["bias_done"].up)

                        def finish(ch, i, b):
                            pool.wait_ge(*g["z1_done"].at(ch + 1))
                            pool.wait_ge(*g["bias_done"].at(ch + 1))
                            pool.tensor_tensor(z[:, :, :], z[:, :, :], bias[:, :, :], ALU.add).then_inc(*g["z_step"].up)
                            pool.wait_ge(*g["z_step"].at(ch + 1))
                            pool.wait_ge(*g_in[b].at(i + 1))
                            pool.tensor_tensor(z[:, :, :], z[:, :, :], gt[b][:, :, :], ALU.mult).then_inc(*post_done[b].up)

                        def first(x):
                            keys(0), normed_keys(0), bonus_terms(0)
                            pool.wait_ge(*g["nt_done"].at(1))
                            pool.tensor_tensor(ntm[0][:, :, :], ntbd[:, :, :],
                                               con[:, C_LEVEL:C_LEVEL + P].unsqueeze(1).to_broadcast([P, PAIRS, P]),
                                               ALU.mult).then_inc(*g["lev_mask"].up)
                            first_inverse(*x)

                        def period(x, y, zz):
                            for l in range(NL):
                                if l < NL - 1:
                                    level_mask(y[0], l + 1)
                                elif x is not None:
                                    level_mask(x[0], 0), first_inverse(*x)
                                if l == 0 and x is not None:
                                    keys(x[0])
                                if l == 1 and zz is not None:
                                    bonus_and_bias(*zz)
                                if l == 2 and x is not None:
                                    normed_keys(x[0])
                                if l == 3 and x is not None:
                                    bonus_terms(x[0])
                                if l == 5 and zz is not None:
                                    finish(*zz)

                        periods(pool, first, period, lambda x: (bonus_and_bias(*x), finish(*x)))

                    @block.scalar
                    def _(act):
                        def squares(ch):
                            act.wait_ge(*g["kk_done"].at(ch + 1))
                            act.activation(sq[:, :, :], kk[:, :, :], ACT.Square).then_inc(*g["sq_done_w"].up)

                        def norm_root(ch):
                            act.wait_ge(*g["mx_done"].at(ch + 1))
                            act.activation(rn[:, :, :], rn[:, :, :], ACT.Sqrt).then_inc(*g["rt_done_w"].up)

                        def decays(ch):
                            act.wait_ge(*g["l_done"].at(ch + 1))
                            act.activation(ep[:, :, :], lcum[:, :, :], ACT.Exp, scale=-DEC).then_inc(*g["e_done"].up)
                            act.activation(em[:, :, :], lcum[:, :, :], ACT.Exp, scale=DEC).then_inc(*g["e_done"].up)
                            act.wait_ge(*g["lq_done"].at(ch + 1))
                            act.activation(eq[:, :, :], lprev[:, :, :], ACT.Exp, scale=-DEC).then_inc(*g["eq_done"].up)

                        def end_decay(ch, i, b):
                            act.wait_ge(*g["e_done"].at(2 * ch + 2))
                            if not (isinstance(ch, int) and ch == 0):
                                act.wait_ge(*g["s_done"].at(ch - 1))
                            act.activation(pend[b][:, :].unsqueeze(2), ep[:, :, CHUNK - 1:CHUNK], ACT.Copy).then_inc(*g["pend_done"].up)

                        def diagonal(ch, i, b, which):
                            act.wait_ge(*g["ar_done"].at(2 * ch + 2))
                            act.wait_ge(*chunk_used[b].at(i))
                            for hs, dst in halves((abd, rbd)[which][b]):
                                last = act.activation(dst, ar[hs, :, which, :], ACT.Copy)
                            last.then_inc(*g["bd_done"].up)

                        def values_out(ch, i, b):
                            act.wait_ge(*g["v_tok"].at(ch + 1))
                            act.wait_ge(*chunk_used[b].at(i))
                            act.activation(vtok[b][:, :, :], bank(6), ACT.Copy).then_inc(*g["v_out"].up)

                        def token_out(ch, i, b, which):
                            act.wait_ge(*g[("b_tok", "k_tok")[which]].at(ch + 1))
                            for hs, dst in halves((btok, ktok)[which][b]):
                                last = act.activation(dst, ps[hs, 6, :].rearrange("p (a n) -> p a n", n=CHUNK), ACT.Copy)
                            last.then_inc(*g[("b_out", "k_out")[which]].up)

                        def level(ch, b, l, q):
                            pairs = slice(q * QP, (q + 1) * QP)
                            act.wait_ge(*g["tr_done"].at(2 * (NL - 1) * ch + 2 * l + q - 1))
                            if l < NL - 1:
                                act.activation(tbd[:, pairs, :], group(q), ACT.Copy)
                            act.activation(inv[b][:, pairs, :], group(2 + q), ACT.Copy).then_inc(*g["t_done"].up)

                        def square(ch):
                            act.wait_ge(*g["yc_done"].at(ch + 1))
                            act.activation(ysq[:, :, :], yc[:, :, :], ACT.Square).then_inc(*g["ysq_done"].up)

                        def root(ch):
                            act.wait_ge(*g["var_done"].at(ch + 1))
                            act.activation(var[:, :], var[:, :], ACT.Sqrt, scale=1.0 / HEAD,
                                           bias=con[:, C_GNEPS:C_GNEPS + 1]).then_inc(*g["yrt_done"].up)

                        def first(x):
                            squares(0), norm_root(0), decays(0), end_decay(*x), diagonal(*x, 0), diagonal(*x, 1)
                            values_out(*x), token_out(*x, 0)

                        def period(x, y, zz):
                            for l in range(NL):
                                if l == 0:
                                    token_out(*y, 1)
                                else:
                                    level(y[0], y[2], l, 0), level(y[0], y[2], l, 1)
                                if l == 0 and x is not None:
                                    squares(x[0])
                                if l == 1 and x is not None:
                                    norm_root(x[0])
                                if l == 2 and x is not None:
                                    decays(x[0])
                                if l == 3 and x is not None:
                                    end_decay(*x), values_out(*x)
                                if l == 4 and zz is not None:
                                    square(zz[0])
                                if l == 4 and x is not None:
                                    diagonal(*x, 0), diagonal(*x, 1), token_out(*x, 0)
                                if l == 5 and zz is not None:
                                    root(zz[0])

                        act.wait_ge(*g["zeros"].at(1))
                        periods(act, first, period, lambda x: (square(x[0]), root(x[0])))

                    @block.tensor
                    def _(pe):
                        def norms(ch):
                            pe.wait_ge(*g["sq_done_w"].at(ch + 1))
                            if not (isinstance(ch, int) and ch < 2):
                                pe.wait_ge(*g["z1_done"].at(ch - 2))
                            pe.matmul(ps[:, 7, :], con[:, C_BLOCK:C_BLOCK + P], flat(sq[:, :, :]),
                                      start=True, stop=True).then_inc(*g["ss_done"].up)

                        def bonus_sums(ch):
                            pe.wait_ge(*g["rk_done"].at(ch + 1))
                            if not (isinstance(ch, int) and ch < 2):
                                pe.wait_ge(*g["yc_done"].at(ch - 1))
                            pe.matmul(ps[:, 7, :], con[:, C_BLOCK:C_BLOCK + P], flat(rk[:, :, :]),
                                      start=True, stop=True).then_inc(*g["bonus_ps"].up)

                        def gram(ch, n):
                            if n == 0:
                                pe.wait_ge(*g["bb_done"].at(ch + 1))
                                pe.wait_ge(*g["g_out"].at(ch))
                            else:
                                pe.wait_ge(*g["kb_done"].at(ch + 1))
                                pe.wait_ge(*g["arb_done"].at(ch + 1))
                            for j in range(PAIRS):
                                ins = pe.matmul(ps[:, 4 + j // 4, (j % 4) * P:(j % 4 + 1) * P], (bbd, kbd)[n][:, j, :],
                                                ar[:, j, :, :].rearrange("p a n -> p (a n)"), start=True, stop=True)
                            ins.then_inc(*g[("g1_done", "g2_done")[n]].up)

                        def by_token(ch, n):
                            if n == 0:
                                pe.wait_ge(*g["v_in"].at(3 * ch + 3))
                                if not (isinstance(ch, int) and ch < 1):
                                    pe.wait_ge(*g["s_step"].at(ch - 1))
                            elif n == 1:
                                pe.wait_ge(*g["bb_done"].at(ch + 1))
                                pe.wait_ge(*g["v_out"].at(ch + 1))
                            else:
                                pe.wait_ge(*g["kb_done"].at(ch + 1))
                                pe.wait_ge(*g["b_out"].at(ch + 1))
                            for j in range(PAIRS):
                                ins = pe.matmul(bank(6)[:, j, :], (vbd, bbd, kbd)[n][:, j, :], idst, start=True, stop=True)
                            ins.then_inc(*g[("v_tok", "b_tok", "k_tok")[n]].up)

                        def level_x(ch, b, l):
                            base = 2 * NL * ch + 2 * l
                            pe.wait_ge(*g["lev_mask"].at(NL * ch + l + 1))
                            for q in range(2):
                                if l == 0:
                                    pe.wait_ge(*g["t_done"].at(2 * (NL - 1) * ch))
                                elif l == 1:
                                    pe.wait_ge(*g["w_done"].at(base - 1 + q))
                                else:
                                    pe.wait_ge(*g["t_done"].at(2 * (NL - 1) * ch + 2 * l - 3 + q))
                                for j in range(QP):
                                    jj = q * QP + j
                                    if l == 0:
                                        ins = pe.transpose(group(q)[:, j, :], ntm[0][:, jj, :], ident)
                                    else:
                                        ins = pe.matmul(group(q)[:, j, :], ntm[l % 2][:, jj, :],
                                                        (wbd if l == 1 else tbd)[:, jj, :], start=True, stop=True)
                                ins.then_inc(*g["x_done_w"].up)

                        def level_t(ch, b, l):
                            base = 2 * NL * ch + 2 * l
                            if l == 1:
                                pe.wait_ge(*g["inv_one"].at(ch + 1))
                            for q in range(2):
                                pe.wait_ge(*g["w_done"].at(base + q + 1))
                                for j in range(QP):
                                    jj = q * QP + j
                                    if l < NL - 1:
                                        pe.matmul(group(q)[:, j, :], inv[b][:, jj, :], wbd[:, jj, :], start=True, stop=True)
                                for j in range(QP):
                                    jj = q * QP + j
                                    ins = pe.matmul(group(2 + q)[:, j, :], wbd[:, jj, :], inv[b][:, jj, :],
                                                    start=True, stop=True)
                                ins.then_inc(*g["tr_done"].up)

                        def solve_x(ch, i, b):
                            pe.wait_ge(*g["s_done"].at(ch))
                            pe.wait_ge(*g["g_out"].at(ch + 1))
                            pe.wait_ge(*g["bd_done"].at(2 * ch + 2))
                            for j in range(PAIRS):
                                pe.matmul(bank(6)[:, j, :], aak[b][:, j, :], vtok[b][:, j, :], start=True, stop=False)
                                ins = pe.matmul(bank(6)[:, j, :], abd[b][:, j, :], state[:, j, :], start=False, stop=True)
                            ins.then_inc(*g["xs_done"].up)

                        def solve_u(ch, i, b):
                            pe.wait_ge(*g["t_done"].at(2 * (NL - 1) * (ch + 1)))
                            pe.wait_ge(*g["xe_done"].at(ch + 1))
                            for j in range(PAIRS):
                                ins = pe.matmul(bank(6)[:, j, :], inv[b][:, j, :], xst[:, j, :], start=True, stop=True)
                            ins.then_inc(*g["us_done"].up)

                        def outputs(ch, i, b):
                            pe.wait_ge(*g["ue_done"].at(ch + 1))
                            for j in range(PAIRS):
                                pe.matmul(bank(7)[:, j, :], rbd[b][:, j, :], state[:, j, :], start=True, stop=False)
                                pe.matmul(bank(7)[:, j, :], ark[b][:, j, :], vtok[b][:, j, :], start=False, stop=False)
                                ins = pe.matmul(bank(7)[:, j, :], arb[b][:, j, :], ust[:, j, :], start=False, stop=True)
                            ins.then_inc(*g["y_done_w"].up)

                        def state_products(ch, i, b):
                            for j in range(PAIRS):
                                pe.matmul(bank(6)[:, j, :], ktok[b][:, j, :], vtok[b][:, j, :], start=True, stop=False)
                                ins = pe.matmul(bank(6)[:, j, :], btok[b][:, j, :], ust[:, j, :], start=False, stop=True)
                            ins.then_inc(*chunk_used[b].up)

                        def by_feature(ch):
                            pe.wait_ge(*g["ybd_done"].at(ch + 1))
                            for j in range(PAIRS):
                                ins = pe.matmul(bank(7)[:, j, :], ybd[:, j, :], idst, start=True, stop=True)
                            ins.then_inc(*g["yf_done"].up)

                        def first(x):
                            norms(0), by_token(0, 0), gram(0, 0)
                            by_token(0, 1), bonus_sums(0), gram(0, 1), by_token(0, 2)

                        def period(x, y, zz):
                            for l in range(NL):
                                level_x(y[0], y[2], l)
                                if l == 1 and x is not None:
                                    norms(x[0])
                                if l == 2 and x is not None:
                                    pe.wait_ge(*g["mx_done"].at(x[0] + 1))
                                if l == 2 and zz is not None:
                                    outputs(*zz)
                                if l == 4 and x is not None:
                                    gram(x[0], 0)
                                if l:
                                    level_t(y[0], y[2], l)
                                if l == 0:
                                    pe.wait_ge(*g["k_out"].at(y[0] + 1))
                                if l == 0 and zz is not None:
                                    solve_x(*zz)
                                if l == 1 and zz is not None:
                                    solve_u(*zz)
                                if l == 2 and zz is not None:
                                    state_products(*zz)
                                if l == 3 and x is not None:
                                    by_token(x[0], 0)
                                if l == 4 and x is not None:
                                    bonus_sums(x[0]), by_token(x[0], 1)
                                if l == 5 and x is not None:
                                    pe.wait_ge(*g["bonus_done"].at(x[0] + 1))
                                    gram(x[0], 1), by_token(x[0], 2)
                                if l == 5 and zz is not None:
                                    by_feature(zz[0])

                        pe.wait_ge(*g["zeros"].at(1))
                        periods(pe, first, period, lambda y: (solve_x(*y), solve_u(*y), outputs(*y), state_products(*y), by_feature(y[0])))

                    @block.vector
                    def _(dve):
                        def begin(ch):
                            dve.wait_ge(*g["tiles_in"].at(4 * ch + 4))
                            dve.tensor_tensor(kk[:, :, :], kt_[:, :, :], column(V_KK), ALU.mult).then_inc(*g["kk_done"].up)
                            dve.scalar_tensor_tensor(k2[:, :, :], at_[:, :, :], 1.0, kt_[:, :, :], ALU.subtract,
                                                     ALU.mult).then_inc(*g["t1_done"].up)
                            dve.tensor_tensor_scan(flat(lcum[:, :, :]), reset[:, :], flat(st_[:, :, :]), 0.0,
                                                   ALU.mult, ALU.add).then_inc(*g["l_done"].up)

                        def bounded(ch):
                            dve.wait_ge(*g["ss_done"].at(ch + 1))
                            dve.tensor_scalar(rn[:, :, :], bank(7), 1e-24, None, ALU.max).then_inc(*g["mx_done"].up)

                        def inverse_norm(ch):
                            dve.wait_ge(*g["rt_done_w"].at(ch + 1))
                            dve.reciprocal(rn[:, :, :], rn[:, :, :]).then_inc(*g["rn_done"].up)

                        def decayed(ch):
                            dve.wait_ge(*g["e_done"].at(2 * ch + 2))
                            dve.tensor_tensor(ar[:, :, 1, :], rt[:, :, :], ep[:, :, :], ALU.mult).then_inc(*g["ar_done"].up)
                            dve.wait_ge(*g["eq_done"].at(ch + 1))
                            dve.wait_ge(*g["kkn_done"].at(ch + 1))
                            dve.scalar_tensor_tensor(ar[:, :, 0, :], kk[:, :, :], -1.0, eq[:, :, :], ALU.mult,
                                                     ALU.mult).then_inc(*g["ar_done"].up)
                            dve.wait_ge(*g["b_done"].at(ch + 1))
                            for hs, dst in halves(bbd):
                                last = dve.tensor_tensor(dst, bb[hs, :, :], em[hs, :, :], ALU.mult)
                            last.then_inc(*g["bb_done"].up)

                        def decayed_keys(ch):
                            dve.wait_ge(*g["k2_done"].at(ch + 1))
                            for hs, dst in halves(kbd):
                                last = dve.tensor_tensor(dst, k2[hs, :, :], em[hs, :, :], ALU.mult)
                            last.then_inc(*g["kb_done"].up)

                        def bonus_value(ch, i, b):
                            dve.wait_ge(*g["bonus_ps"].at(ch + 1))
                            dve.wait_ge(*g["v_in"].at(3 * ch + 3))
                            if not (isinstance(ch, int) and ch < 2):
                                dve.wait_ge(*g["bias_done"].at(ch - 1))
                            dve.tensor_tensor(bonus[b][:, :, :], bank(7), vt_[:, :, :], ALU.mult).then_inc(*g["bonus_done"].up)

                        def masked(out, which, mask):
                            for hs, dst in halves(out):
                                for j in range(2):
                                    src = ps[hs, 4 + j, :].rearrange("p (a s n) -> p a s n", s=2, n=CHUNK)[:, :, which, :]
                                    m = con[hs, mask:mask + CHUNK].unsqueeze(1).to_broadcast([HEAD, 4, CHUNK])
                                    last = dve.tensor_tensor(dst[:, 4 * j:4 * j + 4, :], src, m, ALU.mult)
                            return last

                        def products_b(ch, i, b):
                            dve.wait_ge(*g["g1_done"].at(ch + 1))
                            dve.wait_ge(*g["lev_mask"].at(NL * ch))
                            masked(ntbd, 0, C_STRICT).then_inc(*g["nt_done"].up)
                            dve.wait_ge(*chunk_used[b].at(i))
                            masked(arb[b], 1, C_CAUSAL).then_inc(*g["arb_done"].up)

                        def products_k(ch, i, b):
                            dve.wait_ge(*g["g2_done"].at(ch + 1))
                            dve.wait_ge(*chunk_used[b].at(i))
                            masked(aak[b], 0, C_STRICT)
                            masked(ark[b], 1, C_CAUSAL).then_inc(*g["g_out"].up)

                        def level(ch, l, q):
                            pairs = slice(q * QP, (q + 1) * QP)
                            dve.wait_ge(*g["x_done_w"].at(2 * NL * ch + 2 * l + q + 1))
                            dve.tensor_tensor(wbd[:, pairs, :], group(q), ident.unsqueeze(1).to_broadcast([P, QP, P]),
                                              ALU.add).then_inc(*g["w_done"].up)

                        def take_x(ch):
                            dve.wait_ge(*g["xs_done"].at(ch + 1))
                            dve.tensor_copy(xst[:, :, :], bank(6)).then_inc(*g["xe_done"].up)

                        def take_u(ch):
                            dve.wait_ge(*g["us_done"].at(ch + 1))
                            dve.tensor_copy(ust[:, :, :], bank(6)).then_inc(*g["ue_done"].up)

                        def new_state(ch, i, b):
                            dve.wait_ge(*chunk_used[b].at(i + 1))
                            dve.tensor_tensor(state[:, :, :], bank(6), state[:, :, :], ALU.add).then_inc(*g["s_step"].up)
                            dve.wait_ge(*g["s_step"].at(ch + 1))
                            dve.wait_ge(*g["pend_done"].at(ch + 1))
                            dve.tensor_tensor(state[:, :, :], state[:, :, :], per_pair(pend[b][:, :]), ALU.mult).then_inc(*g["s_done"].up)

                        def centre(ch):
                            dve.wait_ge(*g["y_done_w"].at(ch + 1))
                            dve.tensor_reduce(mean[:, :], bank(7), AX.X, ALU.add).then_inc(*g["m_step"].up)
                            dve.wait_ge(*g["m_step"].at(2 * ch + 1))
                            dve.tensor_scalar(mean[:, :], mean[:, :], -1.0 / HEAD, None, ALU.mult).then_inc(*g["m_step"].up)
                            dve.wait_ge(*g["m_step"].at(2 * ch + 2))
                            dve.tensor_tensor(yc[:, :, :], bank(7), per_pair(mean[:, :]), ALU.add).then_inc(*g["yc_done"].up)

                        def variance(ch):
                            dve.wait_ge(*g["ysq_done"].at(ch + 1))
                            dve.tensor_reduce(var[:, :], ysq[:, :, :], AX.X, ALU.add).then_inc(*g["var_done"].up)

                        def scale(ch):
                            dve.wait_ge(*g["yrt_done"].at(ch + 1))
                            dve.reciprocal(var[:, :], var[:, :]).then_inc(*g["yrn_done"].up)
                            dve.wait_ge(*g["yrn_done"].at(ch + 1))
                            for hs, dst in halves(ybd):
                                last = dve.tensor_tensor(dst, yc[hs, :, :], per_pair(var[:, :])[hs], ALU.mult)
                            last.then_inc(*g["ybd_done"].up)

                        def affine(ch):
                            dve.wait_ge(*g["yf_done"].at(ch + 1))
                            dve.wait_ge(*z_stored.at(ch))
                            dve.tensor_tensor(z[:, :, :], bank(7), column(V_LNW), ALU.mult).then_inc(*g["z1_done"].up)

                        def first(x):
                            begin(0), bounded(0), inverse_norm(0), decayed(0), products_b(*x)
                            decayed_keys(0), bonus_value(*x)

                        def period(x, y, zz):
                            for l in range(NL):
                                level(y[0], l, 0), level(y[0], l, 1)
                                if l == 0 and zz is not None:
                                    take_x(zz[0])
                                if l == 0 and x is not None:
                                    begin(x[0])
                                if l == 1 and zz is not None:
                                    take_u(zz[0])
                                if l == 1 and x is not None:
                                    bounded(x[0])
                                if l == 1:
                                    products_k(*y)
                                if l == 2 and x is not None:
                                    inverse_norm(x[0])
                                if l == 2 and zz is not None:
                                    new_state(*zz)
                                if l == 3 and x is not None:
                                    decayed(x[0])
                                if l == 3 and zz is not None:
                                    centre(zz[0])
                                if l == 4 and x is not None:
                                    products_b(*x), decayed_keys(x[0])
                                if l == 5 and zz is not None:
                                    variance(zz[0])
                                if l == 5 and x is not None:
                                    bonus_value(*x)
                                if l == 5 and zz is not None:
                                    scale(zz[0]), affine(zz[0])

                        dve.wait_ge(*g["zeros"].at(1))
                        dve.wait_ge(*reset_in.at(1))
                        periods(dve, first, period, lambda y: (take_x(y[0]), take_u(y[0]), new_state(*y), centre(y[0]),
                                                               variance(y[0]), scale(y[0]), affine(y[0])))

        def split_phase(hi, lo):
            with ExitStack() as c:
                raw = [sb(f"z_raw{b}", [P, S], c=c) for b in range(2)]
                z_in = [sig(f"z_in{b}", 16) for b in range(2)]
                z_hi, z_lo = sig("z_hi"), sig("z_lo")
                with nc.Block() as block:
                    @block.sync
                    def _(sp):
                        for k in range(KC):
                            if k >= 2:
                                sp.wait_ge(*z_lo.at(k - 1))
                            sp.dma_start(raw[k % 2][:, :].rearrange("p (c n) -> p c n", n=CHUNK),
                                                        t["z_scratch"][:, :, k, :].rearrange("c p n -> p c n")).then_inc(*z_in[k % 2].up)

                    @block.scalar
                    def _(act):
                        for k in range(KC):
                            act.wait_ge(*z_in[k % 2].at(k // 2 + 1))
                            act.activation(hi[:, k, :], raw[k % 2][:, :], ACT.Copy).then_inc(*z_hi.up)

                    @block.vector
                    def _(dve):
                        for k in range(KC):
                            dve.wait_ge(*z_hi.at(k + 1))
                            dve.tensor_tensor(lo[:, k, :], raw[k % 2][:, :], hi[:, k, :].bitcast(F32), ALU.subtract).then_inc(*z_lo.up)
                z_in[0].passed(4), z_in[1].passed(4), z_hi.passed(KC), z_lo.passed(KC)

        def layer1():
            rwkv_projections()
            wkv_phase()
            with ExitStack() as c:
                hi, lo = sb("hi", [P, KC, S], F32R, c), sb("lo", [P, KC, S], F32R, c)
                split_phase(hi, lo)
                with ExitStack() as c2:
                    w = Weights(sb, c2)
                    out_phase(w, t["rk_w_out"], (6 + 2) * KC, hi, lo)
                norm_phase(3, hi, lo)
                ffn_phase(1, hi, lo)

        ada_phase()
        def layer0():
            with ExitStack() as c:
                hi, lo = sb("hi", [P, KC, S], F32R, c), sb("lo", [P, KC, S], F32R, c)
                norm_phase(0, hi, lo)
                with ExitStack() as c2:
                    w = Weights(sb, c2)
                    qk, vt = sb("qk", [P, QCH + KCH, S], c=c2), sb("vt", [P, NT, VDIM], c=c2)
                    with ExitStack() as c3:
                        cos, sin = sb("cos", [P, S], c=c3), sb("sin", [P, S], c=c3)
                        rope_phase(cos, sin)
                        qkv_phase(w, hi, lo, cos, sin, qk, vt)
                    attention_phase(qk, vt, hi, lo)
                    out_phase(w, t["attn_w_out"], 2 * KC, hi, lo)
                norm_phase(1, hi, lo)
                ffn_phase(0, hi, lo)

        layer0()
        layer1()
        with nc.Block() as block:
            stored = sig("stored", 16)

            @block.sync
            def _(sp):
                sp.dma_start(t["outT"], xt[:, :, :]).then_inc(*stored.up)
                sp.wait_ge(*stored.at(1))


def constants():
    con = np.zeros((P, C_ALL), np.float32)
    r = np.arange(P)
    con[:, C_IDENT:C_IDENT + P] = np.eye(P)
    con[:, C_ONES:C_ONES + P] = 1.0
    con[:, C_BLOCK:C_BLOCK + P] = r[:, None] // HEAD == r[None, :] // HEAD
    for m in r:
        if m % HEAD < HEAD // 2:
            con[m + HEAD // 2, C_ROT + m] = -1.0
        else:
            con[m - HEAD // 2, C_ROT + m] = 1.0
    i, j = (r % CHUNK)[:, None], np.arange(CHUNK)[None, :]
    con[:, C_IDST:C_IDST + CHUNK] = i == j
    con[:, C_STRICT:C_STRICT + CHUNK] = j > i
    con[:, C_CAUSAL:C_CAUSAL + CHUNK] = j >= i
    con[:, C_RESET:C_RESET + HALF] = np.arange(HALF) % CHUNK != 0
    chunk = np.arange(BAND)[None, :] // CHUNK - (r // CHUNK)[:, None]
    con[:, C_BAND:C_BAND + BAND] = np.where((chunk >= 0) & (chunk <= 1), 0.0, NEG)
    for n, size in enumerate(LEVELS):
        src, dst = r[:, None], r[None, :]
        con[:, C_LEVEL + n * P:C_LEVEL + (n + 1) * P] = ((src // (2 * size) == dst // (2 * size))
                                                        & (src // size % 2 == 0) & (dst // size % 2 == 1))
    freq = np.float32(10000.0) ** (-np.arange(0, HEAD, 2, dtype=np.float32) / np.float32(HEAD))
    con[:, C_FREQ] = freq[r % (HEAD // 2)]
    con[:, C_EPS] = EPS
    con[:, C_GNEPS] = GN_EPS
    return con


def layout(x, c, positions, ada_w, ada_b, norm1_g, norm2_g,
           attn_w_in, attn_w_out, attn_q_norm, attn_k_norm, attn_sinks,
           rk_mu, rk_w_rkv, rk_w0, rk_w1, rk_w2, rk_a0, rk_a1, rk_a2,
           rk_v0, rk_v1, rk_v2, rk_g1, rk_g2, rk_k_k, rk_k_a, rk_r_k,
           rk_ln_w, rk_ln_b, rk_w_out, ffn_w_in, ffn_w_out):
    def cols(v):
        return np.asarray(v).reshape(-1, P).T

    def tiles(m):
        k, n = m.shape
        return np.ascontiguousarray(m.reshape(k // P, P, n // P, P).transpose(2, 1, 0, 3))

    order = [GROUP * (2 * (j // GROUP) + s) + j % GROUP for j in range(QCH) for s in range(2)]
    sinks = np.asarray(attn_sinks[0])
    w_in = np.asarray(attn_w_in[0])
    wq = w_in[:, :D].reshape(D, 16, HEAD)[:, order].reshape(D, D)
    wk, wv = w_in[:, D:D + VDIM], w_in[:, D + VDIM:]
    w_out = np.asarray(attn_w_out[0]).reshape(16, HEAD, D)[order].reshape(D, D)
    vecs = np.concatenate(
        [cols(ada_b), np.concatenate([cols(g[l]) for l in range(DEPTH) for g in (norm1_g, norm2_g)], 1),
         cols(rk_mu[0]), cols(rk_w0[0]), cols(rk_a0[0]), cols(rk_k_k[0]), cols(rk_k_a[0]), cols(rk_r_k[0]),
         cols(rk_ln_w[0]), cols(rk_ln_b[0])]
        + [cols(np.tile(attn_q_norm[0], 2))] * QCH + [cols(np.tile(attn_k_norm[0], 2))] * KCH
        + [cols(c[0]), np.broadcast_to(sinks, (P, 16))], 1)

    def padded(m, rows, columns):
        out = np.zeros((rows, columns), m.dtype)
        out[:m.shape[0], :m.shape[1]] = m
        return out

    lora1 = [padded(np.asarray(m[0]), D, P) for m in (rk_w1, rk_a1, rk_g1)]
    lora2 = [padded(np.asarray(m[0]), P, D) for m in (rk_w2, rk_a2, rk_g2)]
    ffn_in = np.asarray(ffn_w_in).reshape(DEPTH, KC, P, 2, FITER * FS, P).transpose(0, 4, 2, 1, 3, 5)
    ffn_out = np.asarray(ffn_w_out).reshape(DEPTH, FITER, FS, P, D).transpose(0, 1, 3, 2, 4)
    arrays = {
        "xT": np.asarray(x[0]).T.reshape(KC, P, S).transpose(1, 0, 2),
        "positions": np.broadcast_to(np.asarray(positions), (P, S)),
        "vecs": vecs,
        "consts": constants(),
        "ada_w": np.asarray(ada_w).reshape(DEPTH, KC, P, 6, D).transpose(0, 3, 2, 1, 4).reshape(DEPTH * 6, P, KC, D),
        "wqk": tiles(np.concatenate([wq, wk], 1)),
        "wv": tiles(wv),
        "attn_w_out": tiles(w_out),
        "w_rkv": np.concatenate([tiles(np.asarray(rk_w_rkv[0][p])) for p in range(3)]),
        "lora1": np.concatenate([tiles(m) for m in lora1]),
        "lora2": np.stack([m.reshape(P, KC, P) for m in lora2]),
        "rk_w_out": tiles(np.asarray(rk_w_out[0])),
        "ffn_w_in": ffn_in.reshape(DEPTH * FITER * FS, P, KC, 2 * P),
        "ffn_w_out": ffn_out.reshape(DEPTH * FITER, P, FS, D),
    }
    return {k: np.ascontiguousarray(v) for k, v in arrays.items()}


def kernel(**inputs):
    import concourse.bacc as bacc
    from concourse.bass_utils import run_bass_kernel_spmd

    arrays = layout(**{k: np.asarray(v) for k, v in inputs.items()})
    nc = bacc.Bacc("TRN2", target_bir_lowering=False, num_devices=1)
    t = {k: nc.dram_tensor(f"in_{k}", a.shape, mybir.dt.from_np(a.dtype), kind="ExternalInput").ap()
         for k, a in arrays.items()}
    t["outT"] = nc.dram_tensor("outT", (P, KC, S), F32, kind="ExternalOutput").ap()
    t["scratch"] = nc.dram_tensor("scratch", (6, S // CHUNK, P, KC, CHUNK), F32, kind="Internal").ap()
    t["z_scratch"] = nc.dram_tensor("z_scratch", (S // CHUNK, P, KC, CHUNK), F32, kind="Internal").ap()
    build_program(nc, t)
    r = run_bass_kernel_spmd(nc, [{f"in_{k}": a for k, a in arrays.items()}], core_ids=[0])
    out = r.results[0]["outT"]
    return np.ascontiguousarray(out.transpose(1, 0, 2).reshape(D, S).T)[None]
```
